# Optimizing a Trainium2 kernel written in Bass

```python
import jax, jax.numpy as jnp
from jax import lax
import numpy as np

D_MODEL = 1024
BATCH = 1
SEQ = 512
DEPTH = 1
DEC_BATCH = 8
DEC_SEQ = 4
PAST_LEN = 1024
PAGE_SIZE = 128

HEAD_DIM = 64
N_Q_HEADS = 8
N_KV_HEADS = 2
Q_PER_KV = N_Q_HEADS // N_KV_HEADS
WINDOW = 128
ATTN_BLOCK = 128
ATTN_WIDTH = N_Q_HEADS * HEAD_DIM
KV_WIDTH = N_KV_HEADS * HEAD_DIM
CONV_WIDTH = D_MODEL // 4
CONV_K = 3
N_MEM = 256
N_MEM_HEADS = 4
MEM_WIDTH = N_MEM_HEADS * HEAD_DIM
MIX_WIDTH = ATTN_WIDTH + CONV_WIDTH + MEM_WIDTH
IN_WIDTH = ATTN_WIDTH + 2 * KV_WIDTH + 3 * CONV_WIDTH + MEM_WIDTH
N_EXPERTS = 32
TOP_K = 4
D_FF = D_MODEL
SWIGLU_LIMIT = 7.0
SWIGLU_ALPHA = 1.702
MOE_BLOCK = 128
EPS = 1e-5
ATTN_SCALE = HEAD_DIM ** -0.5

kernel_name = "hybrid_swa_shortconv_memxattn_moe_step"

def _rms_f32(x):
    xf = x.astype(jnp.float32)
    return xf * lax.rsqrt(jnp.mean(xf * xf, axis=-1, keepdims=True) + EPS)

def rmsnorm(x, g):
    return (_rms_f32(x) * g.astype(jnp.float32)).astype(x.dtype)

def group_norm_concat(parts, g):
    y = jnp.concatenate([_rms_f32(p) for p in parts], axis=-1) * g.astype(jnp.float32)
    return y.astype(parts[0].dtype)

def alibi_slopes(n):
    return 2.0 ** (-8.0 * jnp.arange(1, n + 1, dtype=jnp.float32) / n)

def sink_attend(s, sinks, v, eq):
    sink_b = sinks[:, :, None, None]
    m = jnp.maximum(jnp.max(s, axis=-1, keepdims=True), sink_b)
    p = jnp.exp(s - m)
    denom = jnp.sum(p, axis=-1, keepdims=True) + jnp.exp(sink_b - m)
    return jnp.einsum(eq, (p / denom).astype(v.dtype), v)

def swa_prompt(q, k, v, sinks, slopes):
    B, S = q.shape[0], q.shape[1]
    L = ATTN_BLOCK
    nb = S // L
    qb = q.reshape(B, nb, L, N_KV_HEADS, Q_PER_KV, HEAD_DIM)
    kb = k.reshape(B, nb, L, N_KV_HEADS, HEAD_DIM)
    vb = v.reshape(B, nb, L, N_KV_HEADS, HEAD_DIM)
    pad = ((0, 0), (1, 0), (0, 0), (0, 0), (0, 0))
    kk = jnp.concatenate([jnp.pad(kb, pad)[:, :-1], kb], axis=2)
    vv = jnp.concatenate([jnp.pad(vb, pad)[:, :-1], vb], axis=2)
    dist = (L + jnp.arange(L))[:, None] - jnp.arange(2 * L)[None, :]
    key_pos = jnp.arange(nb)[:, None] * L - L + jnp.arange(2 * L)[None, :]
    mask = ((dist >= 0) & (dist < WINDOW))[None] & (key_pos >= 0)[:, None, :]
    s = jnp.einsum('bnqkgd,bnskd->bnkgqs', qb, kk).astype(jnp.float32) * ATTN_SCALE
    s = s - slopes[:, :, None, None] * dist.astype(jnp.float32)
    s = jnp.where(mask[None, :, None, None], s, -jnp.inf)
    out = sink_attend(s, sinks, vv, 'bnkgqs,bnskd->bnqkgd')
    return out.reshape(B, S, ATTN_WIDTH)

def swa_decode(q, k_all, v_all, sinks, slopes):
    B, T = q.shape[0], q.shape[1]
    W = k_all.shape[1] - T
    dist = (W + jnp.arange(T))[:, None] - jnp.arange(W + T)[None, :]
    mask = (dist >= 0) & (dist < WINDOW)
    s = jnp.einsum('btkgd,bskd->bkgts', q, k_all).astype(jnp.float32) * ATTN_SCALE
    s = s - slopes[:, :, None, None] * dist.astype(jnp.float32)
    s = jnp.where(mask[None, None, None], s, -jnp.inf)
    out = sink_attend(s, sinks, v_all, 'bkgts,bskd->btkgd')
    return out.reshape(B, T, ATTN_WIDTH)

def mem_kv(mem, g_mem_norm, w_mem_kv):
    B, M, _ = mem.shape
    kv = rmsnorm(mem, g_mem_norm) @ w_mem_kv
    mk, mv = jnp.split(kv, 2, axis=-1)
    return (mk.reshape(B, M, N_MEM_HEADS, HEAD_DIM), mv.reshape(B, M, N_MEM_HEADS, HEAD_DIM))

def mem_attend(q, mk, mv):
    B, T = q.shape[0], q.shape[1]
    s = jnp.einsum('bthd,bmhd->bhtm', q, mk).astype(jnp.float32) * ATTN_SCALE
    w = jax.nn.softmax(s, axis=-1).astype(q.dtype)
    return jnp.einsum('bhtm,bmhd->bthd', w, mv).reshape(B, T, MEM_WIDTH)

def moe(x, w_router, b_router, w_gate_up, b_gate_up, w_down, b_down):
    N, D = x.shape
    logits = (x @ w_router).astype(jnp.float32) + b_router.astype(jnp.float32)
    top_v, top_e = lax.top_k(logits, TOP_K)
    gates = jax.nn.softmax(top_v, axis=-1)
    NK = N * TOP_K
    flat_e = top_e.reshape(NK)
    flat_tok = jnp.arange(NK, dtype=jnp.int32) // TOP_K
    order = jnp.argsort(flat_e)
    sorted_e = flat_e[order]
    counts = jnp.bincount(flat_e, length=N_EXPERTS)
    starts = jnp.cumsum(counts) - counts
    padded = (counts + MOE_BLOCK - 1) // MOE_BLOCK * MOE_BLOCK
    pad_ends = jnp.cumsum(padded)
    pad_starts = pad_ends - padded
    dest_sorted = pad_starts[sorted_e] + jnp.arange(NK, dtype=jnp.int32) - starts[sorted_e]
    n_blocks = -(-NK // MOE_BLOCK) + N_EXPERTS
    rows = n_blocks * MOE_BLOCK
    row_tok = jnp.zeros((rows,), jnp.int32).at[dest_sorted].set(flat_tok[order])
    block_e = jnp.minimum(jnp.searchsorted(pad_ends, jnp.arange(n_blocks) * MOE_BLOCK, side='right'), N_EXPERTS - 1)
    xs = x[row_tok].reshape(n_blocks, MOE_BLOCK, D)

    def expert_block(args):
        xb, e = args
        h = xb @ w_gate_up[e] + b_gate_up[e]
        gate = jnp.minimum(h[:, 0::2], SWIGLU_LIMIT)
        up = jnp.clip(h[:, 1::2], -SWIGLU_LIMIT, SWIGLU_LIMIT)
        glu = gate * jax.nn.sigmoid(gate * SWIGLU_ALPHA)
        return ((up + 1.0) * glu) @ w_down[e] + b_down[e]

    outs = lax.map(expert_block, (xs, block_e)).reshape(rows, D)
    dest = jnp.zeros((NK,), jnp.int32).at[order].set(dest_sorted)
    picked = outs[dest].reshape(N, TOP_K, D)
    return jnp.sum(picked * gates[..., None].astype(x.dtype), axis=1)

def layer(x, mk, mv, win_k, win_v, conv_prev, g_attn_norm, w_in, conv_w, attn_sinks, g_mix_out, w_out,
          g_ffn_norm, w_router, b_router, w_gate_up, b_gate_up, w_down, b_down):
    B, T, _ = x.shape
    xn = rmsnorm(x, g_attn_norm)
    z = xn @ w_in
    c0 = ATTN_WIDTH
    c1 = c0 + KV_WIDTH
    c2 = c1 + KV_WIDTH
    c3 = c2 + CONV_WIDTH
    c4 = c3 + CONV_WIDTH
    c5 = c4 + CONV_WIDTH
    q, k, v, cb, cc, cv, mq = jnp.split(z, [c0, c1, c2, c3, c4, c5], axis=-1)
    q = q.reshape(B, T, N_KV_HEADS, Q_PER_KV, HEAD_DIM)
    k = k.reshape(B, T, N_KV_HEADS, HEAD_DIM)
    v = v.reshape(B, T, N_KV_HEADS, HEAD_DIM)
    slopes = alibi_slopes(N_Q_HEADS).reshape(N_KV_HEADS, Q_PER_KV)
    sinks = attn_sinks.astype(jnp.float32).reshape(N_KV_HEADS, Q_PER_KV)
    if win_k is None:
        attn = swa_prompt(q, k, v, sinks, slopes)
        k_all, v_all, keep = k, v, WINDOW
        conv_prev = jnp.zeros((B, CONV_K - 1, CONV_WIDTH), x.dtype)
    else:
        k_all = jnp.concatenate([win_k, k], axis=1)
        v_all = jnp.concatenate([win_v, v], axis=1)
        attn = swa_decode(q, k_all, v_all, sinks, slopes)
        keep = win_k.shape[1]
    new_wk = k_all[:, -keep:]
    new_wv = v_all[:, -keep:]
    u_all = jnp.concatenate([conv_prev, cc * cv], axis=1)
    conv_y = conv_w[0] * u_all[:, 0:T]
    for j in range(1, CONV_K):
        conv_y = conv_y + conv_w[j] * u_all[:, j:j + T]
    conv_out = cb * conv_y
    new_conv = u_all[:, -(CONV_K - 1):]
    cross = mem_attend(mq.reshape(B, T, N_MEM_HEADS, HEAD_DIM), mk, mv)
    mix = group_norm_concat([attn, conv_out, cross], g_mix_out)
    h = x + mix @ w_out
    hn = rmsnorm(h, g_ffn_norm).reshape(B * T, D_MODEL)
    y = h + moe(hn, w_router, b_router, w_gate_up, b_gate_up, w_down, b_down).reshape(B, T, D_MODEL)
    return y, new_wk, new_wv, new_conv

def setup_inputs(seed: int = 0) -> dict:
    key = jax.random.key(seed)
    ks = jax.random.split(key, 24)
    f32 = jnp.float32
    win_len = min(WINDOW, PAST_LEN)

    def nrm(k, shape, scale):
        return jax.random.normal(k, shape, f32) * scale

    return {
        'x_prompt': nrm(ks[0], (BATCH, SEQ, D_MODEL), 1.0),
        'x_sample': nrm(ks[1], (DEC_BATCH, DEC_SEQ, D_MODEL), 1.0),
        'mem_prompt': nrm(ks[2], (BATCH, N_MEM, D_MODEL), 1.0),
        'cache_win_k': nrm(ks[3], (DEPTH, DEC_BATCH, win_len, N_KV_HEADS, HEAD_DIM), 1.0),
        'cache_win_v': nrm(ks[4], (DEPTH, DEC_BATCH, win_len, N_KV_HEADS, HEAD_DIM), 1.0),
        'state_conv': nrm(ks[5], (DEPTH, DEC_BATCH, CONV_K - 1, CONV_WIDTH), 1.0),
        'cache_mem_k': nrm(ks[6], (DEPTH, DEC_BATCH, N_MEM, N_MEM_HEADS, HEAD_DIM), 1.0),
        'cache_mem_v': nrm(ks[7], (DEPTH, DEC_BATCH, N_MEM, N_MEM_HEADS, HEAD_DIM), 1.0),
        'g_attn_norm': 1.0 + nrm(ks[8], (DEPTH, D_MODEL), 0.01),
        'w_in': nrm(ks[9], (DEPTH, D_MODEL, IN_WIDTH), D_MODEL ** -0.5),
        'conv_w': nrm(ks[10], (DEPTH, CONV_K, CONV_WIDTH), CONV_K ** -0.5),
        'attn_sinks': nrm(ks[11], (DEPTH, N_Q_HEADS), 0.5),
        'g_mem_norm': 1.0 + nrm(ks[12], (DEPTH, D_MODEL), 0.01),
        'w_mem_kv': nrm(ks[13], (DEPTH, D_MODEL, 2 * MEM_WIDTH), D_MODEL ** -0.5),
        'g_mix_out': 1.0 + nrm(ks[14], (DEPTH, MIX_WIDTH), 0.01),
        'w_out': nrm(ks[15], (DEPTH, MIX_WIDTH, D_MODEL), MIX_WIDTH ** -0.5),
        'g_ffn_norm': 1.0 + nrm(ks[16], (DEPTH, D_MODEL), 0.01),
        'w_router': nrm(ks[17], (DEPTH, D_MODEL, N_EXPERTS), D_MODEL ** -0.5),
        'b_router': nrm(ks[18], (DEPTH, N_EXPERTS), 0.01),
        'w_gate_up': nrm(ks[19], (DEPTH, N_EXPERTS, D_MODEL, 2 * D_FF), D_MODEL ** -0.5),
        'b_gate_up': nrm(ks[20], (DEPTH, N_EXPERTS, 2 * D_FF), 0.01),
        'w_down': nrm(ks[21], (DEPTH, N_EXPERTS, D_FF, D_MODEL), D_FF ** -0.5),
        'b_down': nrm(ks[22], (DEPTH, N_EXPERTS, D_MODEL), 0.01),
        'g_final': 1.0 + nrm(ks[23], (D_MODEL,), 0.01),
    }

def reference(x_prompt, x_sample, mem_prompt, cache_win_k, cache_win_v, state_conv, cache_mem_k, cache_mem_v,
              g_attn_norm, w_in, conv_w, attn_sinks, g_mem_norm, w_mem_kv, g_mix_out, w_out, g_ffn_norm,
              w_router, b_router, w_gate_up, b_gate_up, w_down, b_down, g_final):
    yp, ys = x_prompt, x_sample
    wkp_l, wvp_l, cp_l, mkp_l, mvp_l, wks_l, wvs_l, cs_l = [], [], [], [], [], [], [], []
    for l in range(DEPTH):
        mk_p, mv_p = mem_kv(mem_prompt, g_mem_norm[l], w_mem_kv[l])
        yp, wkp, wvp, cp = layer(yp, mk_p, mv_p, None, None, None,
                                 g_attn_norm[l], w_in[l], conv_w[l], attn_sinks[l], g_mix_out[l], w_out[l],
                                 g_ffn_norm[l], w_router[l], b_router[l], w_gate_up[l], b_gate_up[l],
                                 w_down[l], b_down[l])
        ys, wks, wvs, cs = layer(ys, cache_mem_k[l], cache_mem_v[l], cache_win_k[l], cache_win_v[l], state_conv[l],
                                 g_attn_norm[l], w_in[l], conv_w[l], attn_sinks[l], g_mix_out[l], w_out[l],
                                 g_ffn_norm[l], w_router[l], b_router[l], w_gate_up[l], b_gate_up[l],
                                 w_down[l], b_down[l])
        wkp_l.append(wkp)
        wvp_l.append(wvp)
        cp_l.append(cp)
        mkp_l.append(mk_p)
        mvp_l.append(mv_p)
        wks_l.append(wks)
        wvs_l.append(wvs)
        cs_l.append(cs)
    y_prompt = rmsnorm(yp, g_final)
    y_sample = rmsnorm(ys, g_final)
    return (y_prompt, y_sample,
            jnp.stack(wkp_l), jnp.stack(wvp_l), jnp.stack(cp_l), jnp.stack(mkp_l), jnp.stack(mvp_l),
            jnp.stack(wks_l), jnp.stack(wvs_l), jnp.stack(cs_l))


_drawn_inputs = setup_inputs


def setup_inputs(seed=0):
    import zlib

    import numpy as np

    out = dict(_drawn_inputs(seed))
    spreads = {}
    factors = {'g_mem_norm': 2.885, 'b_gate_up': 8.0, 'b_down': 8.0, 'g_final': 5.795}
    for name, (base, spread) in spreads.items():
        noise = np.random.default_rng([zlib.crc32(name.encode()), seed]).standard_normal(out[name].shape)
        drawn = base * np.exp(spread * noise) if base else spread * noise
        out[name] = __import__('jax').numpy.asarray(drawn.astype(out[name].dtype))
    for name, factor in factors.items():
        out[name] = (out[name] * factor).astype(out[name].dtype)
    return out
```

```python
from contextlib import ExitStack

import numpy as np

import concourse.bass as bass
from concourse import mybir

F32 = mybir.dt.float32
I32 = mybir.dt.int32
U32 = mybir.dt.uint32
ALU = mybir.AluOpType
ACT = mybir.ActivationFunctionType
AX = mybir.AxisListType

P = 128
D = 1024
KD = D // P
NPR, NB, TS = 512, 8, 4
NSM = NB * TS
NT = NPR + NSM
NTT = 5
HD = 64
WIN = 128
NMEM = 256
NE, TOPK = 32, 4
LIMIT, ALPHA = 7.0, 1.702
EPS = 1e-5
SCALE = HD ** -0.5
ROWS = [P, P, P, P, NSM]
HALF = NT // 2
BIG = -1e30

CAP = 104
EXTRA = 20
UB = 4
NCH = 6
RING = 8
CHW = 4096
assert NE % UB == 0 and EXTRA % UB == 0 and (UB * NCH) % RING == 0
BLOCKS = -(-NT // CAP)
assert EXTRA >= (NT * TOPK) // CAP

_C = {}
_n = 0
for _name, _w in (("ident", P), ("tri", P), ("ones", P), ("dist", 256), ("sbias", 320), ("slot", CAP),
                  ("tokid", NTT), ("pad", 1), ("sel", 8), ("valid", NTT), ("iota", NE), ("blk", EXTRA),
                  ("mhalf", 16)):
    _C[_name] = (_n, _n + _w)
    _n += _w
NCONST = _n


def constants():
    c = np.zeros((P, NCONST), np.float32)
    p = np.arange(P)

    def put(name, v):
        c[:, slice(*_C[name])] = v

    put("ident", np.eye(P))
    put("tri", p[:, None] < p[None, :])
    put("ones", 1.0)
    dist = (P + p)[:, None] - np.arange(256)[None, :]
    put("dist", np.where((dist >= 0) & (dist < WIN), -dist, BIG))
    sb = np.zeros((P, 2, 160), np.float32)
    for r in range(2):
        for row in range(P):
            b, head, t = 4 * r + row // 32, (row // 4) % 8, row % 4
            slope = 2.0 ** -(head + 1)
            dc = WIN + t - np.arange(WIN)
            sb[row, r, :WIN] = np.where(dc < WIN, -slope * dc / SCALE, BIG)
            for j in range(NSM):
                ok = j // TS == b and j % TS <= t
                sb[row, r, WIN + j] = -slope * (t - j % TS) / SCALE if ok else BIG
    put("sbias", sb.reshape(P, 320))
    put("slot", np.arange(CAP)[None, :])
    put("tokid", P * np.arange(NTT)[None, :] + p[:, None])
    put("pad", (NT + p)[:, None])
    put("sel", (p[:, None] // 4) % 8 == np.arange(8)[None, :])
    put("valid", np.arange(NTT)[None, :] * P + p[:, None] < NT)
    put("iota", np.arange(NE)[None, :])
    put("blk", np.arange(EXTRA)[None, :])
    put("mhalf", -0.5)
    return c


def build(nc, x_prompt, x_sample, mem_prompt, cache_win_k, cache_win_v, win_kT, mem_kT, cache_mem_v,
          vectors, w_in, attn_sinks, w_mem_kv, w_out, w_router, b_router, w_gate_up, biases_up, w_down, biases_down,
          g_final,
          y_prompt, y_sample, o_wkp, o_wvp, o_convp, o_mkp, o_mvp, o_wks, o_wvs, o_convs):
    ctx = ExitStack()
    with ctx:
        const_dram = nc.inline_tensor(constants(), name="shape_constants")
        const_dram = const_dram.ap() if hasattr(const_dram, "ap") else const_dram
        hn_tbl = nc.dram_tensor("hn_tbl", (NT, D), F32, kind="Internal").ap()
        y_tbl = nc.dram_tensor("y_tbl", (NT + CAP, D), F32, kind="Internal").ap()

        def sb(name, w, dt=F32):
            return ctx.enter_context(nc.sbuf_tensor(name, [P, w], dt))

        sems = {}

        def sem(name):
            if name not in sems:
                sems[name] = ctx.enter_context(nc.semaphore(name))
            return sems[name]

        ring = sb("ring", RING * CHW)
        area = sb("area", 8192 + 13 * NT)
        cst = sb("cst", NCONST)
        vecs = sb("vecs", 70)
        bgu_t = sb("bgu", 2 * NE * KD)
        bd = sb("bd", NE * KD)
        wr_t = sb("wr", KD * NE)
        brt = sb("brt", NE)
        small = sb("small", 200)
        us_t = sb("us", 2 * NB * 6)
        lg_t = sb("lg", NTT * NE)
        flag_i = sb("flag_i", 1, I32)
        eid_i = sb("eid_i", EXTRA + 1, I32)
        idx_i = sb("idx_i", UB, I32)

        def c_(name, rows=P):
            a, b = _C[name]
            return cst[0:rows, a:b]

        ident = c_("ident")

        def view(t, off, shape):
            n = int(np.prod(shape))
            names = " ".join(f"d{i}" for i in range(len(shape)))
            ap = t[:, off:off + n]
            if len(shape) == 1:
                return ap
            return ap.rearrange(f"p ({names}) -> p {names}", **{f"d{i}": s for i, s in enumerate(shape)})

        xrow = view(area, 0, [NTT, D])
        memrow = view(area, NTT * D, [2, D])
        junk = view(area, 7 * D, [D])
        wo = view(area, 0, [KD, D])
        zT = view(area, 8192, [13, NT])
        memT = view(area, 8192, [KD, NMEM])
        END = RING * CHW
        wi_off = END - KD * 1792
        wi = view(ring, wi_off, [KD, 1792])
        xT0 = view(ring, wi_off - KD * NT, [KD, NT])
        wm = view(ring, wi_off - KD * NT - KD * 512, [KD, 512])
        S_OFF = wi_off - KD * NT - 6144
        Sb = view(ring, S_OFF, [2, 2048])
        pT = view(ring, S_OFF + 4096, [4, 512])
        o = S_OFF + 6144
        mckT = view(ring, o, [2, NB, 256])
        mcv = view(ring, o + 4096, [NB, 2, 256])
        kcT = view(ring, o + 8192, [NB, P])
        vc = view(ring, o + 9216, [NB, P])
        qbd = view(ring, o + 14080, [NB, 2, 16])
        mqbd = view(ring, o + 14336, [2, NB, 8])
        ST = view(ring, o + 14464, [256])
        ul = view(ring, o + 14720, [2, 18])
        ulr = view(ring, o + 14756, [2, P])
        assert o + 15012 <= END
        sq = view(ring, END - 8 * NT, [8, NT])
        h_off = END - 8 * NT - 8192
        xr = view(ring, h_off, [2, D])
        hrow = view(ring, h_off + 2048, [2, D])
        hnr = view(ring, h_off + 4096, [2, D])
        hnT = view(ring, h_off + 6144, [2, KD, P])
        junk_h = view(ring, 4 * CHW, [D])
        assert h_off >= 4 * CHW - 256
        a = [0]

        def moe_buf(shape):
            v = view(area, a[0], shape)
            a[0] += int(np.prod(shape))
            return v

        xg = moe_buf([2, D])
        xTe = moe_buf([2, KD, CAP])
        act = moe_buf([2, KD, CAP])
        raw = moe_buf([2, 4, CAP])
        sig = moe_buf([2, 2, CAP])
        yT = moe_buf([2, KD, CAP])
        yrow = moe_buf([2, D])
        hot = moe_buf([2, NTT, CAP])
        gfin = moe_buf([D])
        NVC = NE + EXTRA + 1
        a_route = a[0]
        posm = moe_buf([NTT, NVC])
        gate = moe_buf([NTT, NVC])
        rv = moe_buf([2, NTT, 3])
        gcol = moe_buf([UB])
        cnt = moe_buf([NE])
        wk2 = moe_buf([2])
        nbig = max(NTT * TOPK, EXTRA) * NE
        big1, big2, big3 = (view(area, i * nbig, [nbig]) for i in range(3))
        wk = view(area, 4096, [12, 160])
        assert a[0] <= 8192 + 13 * NT, a[0]
        assert 3 * nbig <= 4096
        yf = view(ring, 0, [NTT, D])
        jf = view(ring, NTT * D, [D])

        kvr = view(ring, CHW, [NTT, 256])
        mkT = view(ring, CHW + 1280, [2, 256])
        mkv = view(ring, CHW + 1792, [2, 512])
        assert CHW + 2816 <= S_OFF
        bgu = bgu_t[:, :].rearrange("p (s n) -> p s n", s=2)
        wr = wr_t[:, :].rearrange("p (k e) -> p k e", k=KD)
        us = us_t[:, :].rearrange("p (c b r) -> p c b r", c=2, b=NB)
        lg = lg_t[:, :].rearrange("p (j e) -> p j e", j=NTT)
        ss7, ms7, rs7 = small[:, 0:7], small[:, 8:15], small[:, 16:23]
        sink = small[:, 24:34]
        mx, negm, sarg = small[:, 34:42], small[:, 42:58], small[:, 58:74]
        rsum, esum, rinv = small[:, 74:90], small[:, 90:106], small[:, 106:122]
        ss3, rs3 = small[:, 122:137], small[:, 137:152]
        ssh, rsh = small[:, 152:157], small[:, 157:162]
        ssf, rsf = small[:, 162:167], small[:, 167:172]
        sink8 = small[:, 172:182]
        selt = small[:, 182:190]
        mxh = small[:, 190:191]

        G_ATTN, G_MEM, G_MIX, G_FFN, CONVW, STATE = 0, 8, 16, 24, 32, 38

        psum = ctx.enter_context(nc.psum_tensor("psum", [P, 8 * 512], F32))
        banks = [psum[:, i * 512:(i + 1) * 512] for i in range(8)]

        def wait(eng, name, value):
            if not isinstance(value, int) or value > 0:
                eng.wait_ge(sem(name), value)

        def split(ap, n):
            return ap.rearrange("p (a b) -> p a b", a=n)

        def row_tile(r):
            return (memrow[:, r, :], P) if r < 2 else (xrow[0:ROWS[r - 2], r - 2, :], ROWS[r - 2])

        WCOL = {0: 0, 1: 128, 2: 256, 3: 384, 4: 768, 5: 896, 6: 1536, 7: 1664, 8: 512, 9: 1024, 10: 1152, 11: 1280, 12: 1408}
        Z_FIRST = [8, 0, 1, 2, 3]
        Z_LATER = [[9, 11], [10, 12], [4, 5], [6, 7]]
        Z_ORDER = Z_FIRST + [t for g in Z_LATER for t in g]
        NZ1 = 2 * len(Z_FIRST)
        UNITS = [("swa", n, 8, 256 if n else P) for n in range(4)] + \
                [("mem", n, 4, 256) for n in range(4)] + [("sswa", 0, 2, 160), ("smem", 0, 1, 256)]
        NU = len(UNITS)
        NJ = [3] + [5] * 3 + [3] * 4 + [2, 2]
        JB = [sum(NJ[:i]) for i in range(NU + 1)]
        S_BANK = [0, 0, 0, 0, 0, 2, 0, 2, 0, 2]

        def s_view(i):
            kind, n, nh, w = UNITS[i]
            return Sb[:, i % 2, 0:nh * w].rearrange("p (h k) -> p h k", h=nh)

        def s_psum(i):
            kind, n, nh, w = UNITS[i]
            if kind == "mem":
                return psum[:, S_BANK[i] * 512:(S_BANK[i] + 2) * 512].rearrange("p (h k) -> p h k", k=256)
            return banks[S_BANK[i]][:, 0:nh * w].rearrange("p (h k) -> p h k", h=nh)

        def swa_psum(n, h):
            w = 256 if n else P
            return banks[h // 2][:, (h % 2) * 256:(h % 2) * 256 + w]

        block = ctx.enter_context(nc.Block())

        N_OUT_STORES = 4 + 2 + 2 * NB + 2

        def chunk_slot(u, q):
            return (u * NCH + q) % RING

        USES = UB * NCH // RING

        def chunk_fill(u, q):
            return (u * NCH + q) // RING + 1

        def gu_w(slot):
            return view(ring, slot * CHW, [2, 2, KD, P])

        def dn_w(slot):
            return view(ring, slot * CHW, [4, D])

        @block.sync
        def _(sp):
            sp.dma_start(memrow, mem_prompt[0].rearrange("(m p) d -> p m d", p=P)).then_inc(sem("ld_mem"), 16)
            for j in range(4):
                sp.dma_start(xrow[:, j, :], x_prompt[0, j * P:(j + 1) * P, :]).then_inc(sem(f"ld_x{j}"), 16)
            sp.dma_start(xrow[0:NSM, 4, :], x_sample.rearrange("b t d -> (b t) d")).then_inc(sem("ld_x4"), 16)
            sp.dma_start(wm, w_mem_kv[0].rearrange("(k p) n -> p k n", p=P)).then_inc(sem("ld_wm"), 16)
            sp.dma_start(wi, w_in.rearrange("(k p) n -> p k n", p=P)).then_inc(sem("ld_wi"), 16)

            def load_chunk(e, slot, q):
                src = w_gate_up[e * 4 + q] if q < 4 else w_down[e * 2 + (q - 4)]
                sp.dma_start(view(ring, slot * CHW, [CHW]), src).then_inc(sem(f"chunk{slot}"), 16)

            load_chunk(0, 0, 0)
            sp.wait_ge(sem("xT_pe"), 14)
            sp.dma_start(wo, w_out.rearrange("(k p) n -> p k n", p=P)).then_inc(sem("ld_wo"), 16)
            sp.wait_ge(sem("mkv_ready"), 2)
            for m in range(2):
                sp.dma_start(o_mkp[0, 0, m * P:(m + 1) * P].rearrange("m h d -> m (h d)"),
                             mkv[:, m, 0:256]).then_inc(sem("st_out"), 16)
                sp.dma_start(o_mvp[0, 0, m * P:(m + 1) * P].rearrange("m h d -> m (h d)"),
                             mkv[:, m, 256:512]).then_inc(sem("st_out"), 16)
            sp.wait_ge(sem("kvr_dve"), 3)
            sp.wait_ge(sem("kvr_act"), 2)
            for dst, off in ((o_wkp, 0), (o_wvp, P)):
                sp.dma_start(dst[0, 0].rearrange("s h d -> s (h d)"), kvr[:, 3, off:off + P]).then_inc(sem("st_out"), 16)
            for b in range(NB):
                for dst, off in ((o_wks, 0), (o_wvs, P)):
                    sp.dma_start(dst[0, b, WIN - TS:WIN].rearrange("s h d -> s (h d)"),
                                 kvr[b * TS:(b + 1) * TS, 4, off:off + P]).then_inc(sem("st_out"), 16)
            sp.wait_ge(sem("z_pe"), 26)
            sp.dma_start(kcT, win_kT).then_inc(sem("ld_kc"), 16)
            sp.dma_start(mckT, mem_kT).then_inc(sem("ld_mck"), 16)
            sp.dma_start(vc, cache_win_v[0].rearrange("b s h d -> s b (h d)")).then_inc(sem("ld_vc"), 16)
            sp.dma_start(mcv, cache_mem_v[0].rearrange("b (m p) h d -> p b m (h d)", p=P)).then_inc(sem("ld_mcv"), 16)
            sp.wait_ge(sem("ulr_ready"), 1)
            sp.dma_start(o_convp[0, 0].rearrange("r (c n) -> r c n", c=2), ulr[0:2]).then_inc(sem("st_out"), 16)
            sp.dma_start(o_convs[0].rearrange("b r (c n) -> (b r) c n", c=2), ulr[2:18]).then_inc(sem("st_out"), 16)
            sp.wait_ge(sem("job_pe"), JB[NU])
            sp.wait_ge(sem("st_out"), 16 * N_OUT_STORES)

            def load_x(j):
                src = x_prompt[0, j * P:(j + 1) * P, :] if j < 4 else x_sample.rearrange("b t d -> (b t) d")
                sp.dma_start(xr[0:ROWS[j], j % 2, :], src).then_inc(sem(f"ld_xr{j % 2}"), 16)

            load_x(0)
            load_x(1)
            for q in range(1, 4):
                load_chunk(0, q, q)
            for j in range(NTT):
                sp.wait_ge(sem("h_ready"), 2 * (j + 1))
                if j + 2 < NTT:
                    load_x(j + 2)
                sp.dma_start(y_tbl[j * P:j * P + ROWS[j], :], hrow[0:ROWS[j], j % 2, :]).then_inc(sem(f"st_h{j % 2}"), 16)
                sp.wait_ge(sem("hn_ready"), j + 1)
                sp.dma_start(hn_tbl[j * P:j * P + ROWS[j], :], hnr[0:ROWS[j], j % 2, :]).then_inc(sem(f"st_hn{j % 2}"), 16)
            sp.wait_ge(sem("lg_pe"), NTT)
            sp.wait_ge(sem("sq_pe"), NTT)
            for par, n in ((0, 3), (1, 2)):
                sp.wait_ge(sem(f"st_h{par}"), 16 * n)
                sp.wait_ge(sem(f"st_hn{par}"), 16 * n)
            for q in range(4, NCH):
                load_chunk(0, q, q)
            for q in range(RING - NCH):
                load_chunk(1, NCH + q, q)
            sp.wait_ge(sem("route_ready"), 1)
            flag = sp.value_load(flag_i[0:1, 0:1], min_val=0, max_val=1)

            def refill(base, u, q, expert):
                m = u * NCH + q - RING
                lu, lq = m // NCH, m % NCH
                if lq < 4:
                    sp.wait_ge(sem("gu_pe"), base * 4 + (lu * 4 + lq + 1))
                else:
                    sp.wait_ge(sem("dn_pe"), base * 2 + (lu * 2 + lq - 3))
                load_chunk(expert, chunk_slot(u, q), q)

            for u in range(1, UB):
                for q in range(NCH):
                    if u * NCH + q >= RING:
                        refill(0, u, q, u)
            with sp.Fori(1, NE // UB) as it:
                for u in range(UB):
                    for q in range(NCH):
                        refill(it * UB, u, q, it * UB + u)
            with sp.If(flag > 0):
                with sp.Fori(0, EXTRA // UB) as it:
                    for u in range(UB):
                        e = sp.value_load(eid_i[0:1, bass.ds(it * UB + u, 1)], min_val=0, max_val=NE - 1)
                        for q in range(NCH):
                            refill(it * UB + NE, u, q, e)
            last = flag * EXTRA + NE
            sp.wait_ge(sem("scattered"), (last + 1) * 16)
            for j in range(NTT):
                sp.dma_start(yf[0:ROWS[j], j, :], y_tbl[j * P:j * P + ROWS[j], :]).then_inc(sem(f"ld_y{j}"), 16)
            for j in range(NTT):
                sp.wait_ge(sem("yf_ready"), j + 1)
                dst = y_prompt[0, j * P:(j + 1) * P, :] if j < 4 else y_sample.rearrange("b t d -> (b t) d")
                sp.dma_start(dst, yf[0:ROWS[j], j, :]).then_inc(sem("st_y"), 16)
            sp.wait_ge(sem("st_y"), 16 * NTT)

        @block.gpsimd
        def _(pool):
            pool.wait_ge(sem("ld_cst"), 16)
            mh = c_("mhalf")
            for r in range(7):
                n = row_tile(r)[1]
                pool.wait_ge(sem("ms_ready"), r + 1)
                nc.gpsimd.tensor_tensor(rs7[0:n, r:r + 1], ms7[0:n, r:r + 1], mh[0:n, 0:1], ALU.pow).then_inc(sem("rs_ready"), 1)
            for i, (kind, n, nh, w) in enumerate(UNITS):
                s = s_view(i)
                pool.wait_ge(sem("rinv_ready"), i + 1)
                ri = rinv[:, 8 * (i % 2):8 * (i % 2) + nh].rearrange("p (h o) -> p h o", o=1).broadcast_to([P, nh, w])
                nc.gpsimd.tensor_tensor(s, s, ri, ALU.mult).then_inc(sem("p_ready"), 1)
            pool.wait_ge(sem("ss3_ready"), 1)
            nc.gpsimd.tensor_tensor(rs3, ss3, mh[:, 0:15], ALU.pow).then_inc(sem("rs3_ready"), 1)
            for j in range(NTT):
                pool.wait_ge(sem("ssh_ready"), j + 1)
                nc.gpsimd.tensor_tensor(rsh[0:ROWS[j], j:j + 1], ssh[0:ROWS[j], j:j + 1], mh[0:ROWS[j], 0:1],
                                        ALU.pow).then_inc(sem("rsh_ready"), 1)
            pool.wait_ge(sem("route_ready"), 1)
            pool.dma_start(y_tbl[NT:NT + CAP, :], yrow[0:CAP, 1, :]).then_inc(sem("pad_rows"), 16)
            pool.wait_ge(sem("pad_rows"), 16)
            for par, n in ((0, 3), (1, 2)):
                pool.wait_ge(sem(f"st_h{par}"), 16 * n)
                pool.wait_ge(sem(f"st_hn{par}"), 16 * n)

            bound = pool.alloc_register("bound")
            none = pool.value_load(eid_i[0:1, EXTRA:EXTRA + 1], min_val=0, max_val=0)

            def gather(n, k):
                pool.wait_ge(sem("idx_ready"), n + 1)
                pool.reg_add(bound, none, NT - 1)
                nc.gpsimd.indirect_dma_start(
                    xg[0:CAP, k % 2, :], None, hn_tbl[:, :],
                    bass.IndirectOffsetOnAxis(ap=idx_i[0:CAP, k % UB:k % UB + 1].bitcast(U32), axis=0),
                    bounds_check=bound, oob_is_err=False).then_inc(sem("gathered"), 16)

            def scatter(n, k):
                pool.wait_ge(sem("yrow_ready"), n * 2 + 2)
                wait(pool, "scattered", n * 16)
                pool.reg_add(bound, none, NT + CAP - 1)
                nc.gpsimd.indirect_dma_start(
                    y_tbl[:, :], bass.IndirectOffsetOnAxis(ap=idx_i[0:CAP, (k - 1) % UB:(k - 1) % UB + 1].bitcast(U32), axis=0),
                    yrow[0:CAP, (k - 1) % 2, :], None,
                    bounds_check=bound, oob_is_err=True, compute_op=ALU.add).then_inc(sem("scattered"), 16)

            flag = pool.value_load(flag_i[0:1, 0:1], min_val=0, max_val=1)
            gather(0, 0)
            for u in range(UB):
                scatter(u, u)
                gather(u + 1, u + 1)
            with pool.Fori(1, NE // UB) as it:
                for u in range(UB):
                    scatter(it * UB + u, u)
                    gather(it * UB + (u + 1), u + 1)
            with pool.If(flag > 0):
                with pool.Fori(0, EXTRA // UB) as it:
                    for u in range(UB):
                        scatter(it * UB + (NE + u), u)
                        gather(it * UB + (NE + u + 1), u + 1)
            last = flag * EXTRA + NE
            scatter(last, 0)
            for j in range(NTT):
                pool.wait_ge(sem("ssf_ready"), j + 1)
                nc.gpsimd.tensor_tensor(rsf[0:ROWS[j], j:j + 1], ssf[0:ROWS[j], j:j + 1], mh[0:ROWS[j], 0:1],
                                        ALU.pow).then_inc(sem("rsf_ready"), 1)

        @block.scalar
        def _(ac):
            ac.dma_start(cst[:, :], const_dram).then_inc(sem("ld_cst"), 16)
            ac.dma_start(vecs[:, :], vectors).then_inc(sem("ld_vec"), 16)
            ac.dma_start(sink[:, 0:8], attn_sinks[0:1, :].broadcast_to([P, 8])).then_inc(sem("ld_sm"), 16)
            ac.dma_start(brt[:, :], b_router[0:1, :].broadcast_to([P, NE])).then_inc(sem("ld_sm"), 16)
            ac.dma_start(wr, w_router[0].rearrange("(k p) e -> p k e", p=P)).then_inc(sem("ld_sm"), 16)
            ac.dma_start(bgu_t[:, :], biases_up).then_inc(sem("ld_b"), 16)
            ac.dma_start(bd[:, :], biases_down).then_inc(sem("ld_b"), 16)
            for dst, src in ((o_wks, cache_win_k), (o_wvs, cache_win_v)):
                ac.dma_start(dst[0, :, 0:WIN - TS].rearrange("b s h d -> b (s h d)"),
                             src[0, :, TS:WIN].rearrange("b s h d -> b (s h d)")).then_inc(sem("st_win"), 16)

            for r in range(7):
                ap, n = row_tile(r)
                if r == 0:
                    ac.wait_ge(sem("ld_mem"), 16)
                elif r >= 2:
                    ac.wait_ge(sem(f"ld_x{r - 2}"), 16)
                wait(ac, "ss_ready", r)
                nc.scalar.activation(junk[0:n], ap, ACT.Square, accum_out=ss7[0:n, r:r + 1]).then_inc(sem("ss_ready"), 1)
            for m in range(2):
                ac.wait_ge(sem("mkv_pe"), m + 1)
                nc.scalar.copy(mkv[:, m, :], banks[5 + m][:, :]).then_inc(sem("mkv_ready"), 1)
            ac.wait_ge(sem("mkT_pe"), 1)
            nc.scalar.copy(view(ring, CHW + 1280, [512]), banks[7][:, :]).then_inc(sem("mkT_ready"), 1)

            def z_odd(i):
                ac.wait_ge(sem("z_pe"), 2 * i + 2)
                bank = (2 * i + 1) % 8 if 2 * i < NZ1 else 7
                nc.scalar.copy(zT[:, Z_ORDER[i], HALF:NT], banks[bank][:, 0:HALF]).then_inc(sem("z_act"), 1)

            for i in range(len(Z_FIRST)):
                z_odd(i)
            for j in (1, 3):
                c0 = P if j < 3 else 0
                ac.wait_ge(sem("kvr_pe"), j + 1)
                nc.scalar.copy(kvr[0:ROWS[j], j, c0:256], banks[(NZ1 + j) % 8][0:ROWS[j], c0:256]).then_inc(sem("kvr_act"), 1)

            def softmax_exp(i):
                kind, n, nh, w = UNITS[i]
                s, par = s_view(i), 8 * (i % 2)
                ac.wait_ge(sem("negm_ready"), i + 1)
                if kind in ("mem", "smem"):
                    ac.wait_ge(sem("job_pe"), JB[i - 1] - 1)
                if kind in ("swa", "sswa"):
                    nc.scalar.activation(esum[:, par:par + nh], sarg[:, par:par + nh], ACT.Exp)
                for h in range(nh):
                    src = s_psum(i)[:, h, :] if kind in ("mem", "smem") else s[:, h, :]
                    last = nc.scalar.activation(s[:, h, :], src, ACT.Exp, bias=negm[:, par + h:par + h + 1], scale=SCALE,
                                                accum_out=rsum[:, par + h:par + h + 1])
                last.then_inc(sem("exp_ready"), 1)

            def move_out(i):
                kind, n, nh, w = UNITS[i]
                for k in range(NJ[i] - 1):
                    ac.wait_ge(sem("job_pe"), JB[i] + k + 1)
                    bank = banks[4 + (JB[i] + k) % 2]
                    if kind == "swa":
                        g, half = (k, 1) if n == 0 else (k // 2, k % 2)
                        nc.scalar.copy(pT[:, g * 2 + half, :], bank[:, :]).then_inc(sem("job_out"), 1)
                    elif kind == "mem":
                        nc.scalar.copy(pT[:, k, :], bank[:, :]).then_inc(sem("job_out"), 1)
                    elif kind == "sswa":
                        nc.scalar.copy(pT[:, 0, 0:256], bank[:, 0:256])
                        nc.scalar.copy(pT[0:32, 1, 0:256], bank[0:32, 256:512]).then_inc(sem("job_out"), 1)
                    else:
                        nc.scalar.copy(pT[:, 0, 0:256], bank[:, 0:256]).then_inc(sem("job_out"), 1)
                k = JB[i + 1] - 1
                ac.wait_ge(sem("job_pe"), k + 1)
                bank = banks[4 + k % 2]
                if kind == "swa":
                    nc.scalar.copy(zT[:, 0:4, n * P:(n + 1) * P], split(bank[:, :], 4)).then_inc(sem("job_out"), 1)
                elif kind == "mem":
                    nc.scalar.copy(zT[:, 6:8, n * P:(n + 1) * P], split(bank[:, 0:256], 2)).then_inc(sem("job_out"), 1)
                elif kind == "sswa":
                    for g in range(2):
                        rows = slice(g * HD, (g + 1) * HD)
                        src = bank[rows, 0:256].rearrange("p (b v g t) -> p v b g t", b=NB, v=2, g=4)[:, g]
                        dst = zT[rows, 0:4, NPR:NT].rearrange("p g (b t) -> p b g t", b=NB)
                        last = nc.scalar.copy(dst, src)
                    last.then_inc(sem("job_out"), 1)
                else:
                    for g in range(2):
                        rows = slice(g * HD, (g + 1) * HD)
                        src = bank[rows, 0:P].rearrange("p (b c v t) -> p v b c t", b=NB, c=2, v=2)[:, g]
                        dst = zT[rows, 6:8, NPR:NT].rearrange("p c (b t) -> p b c t", b=NB)
                        last = nc.scalar.copy(dst, src)
                    last.then_inc(sem("job_out"), 1)

            zi = len(Z_FIRST)
            for i in range(NU):
                softmax_exp(i)
                if i < 4:
                    for _ in Z_LATER[i]:
                        z_odd(zi)
                        zi += 1
                move_out(i)

            ac.wait_ge(sem("conv_done"), 2)
            ac.wait_ge(sem("job_out"), JB[NU])
            ac.wait_ge(sem("st_out"), 16 * N_OUT_STORES)
            for t in range(8):
                nc.scalar.activation(sq[:, t, :], zT[:, t, :], ACT.Square).then_inc(sem("sq_ready"), 1)
            for j in range(NTT):
                n = ROWS[j]
                ac.wait_ge(sem("h_ready"), 2 * (j + 1))
                wait(ac, "ssh_raw", j)
                nc.scalar.activation(junk_h[0:n], hrow[0:n, j % 2, :], ACT.Square, accum_out=ssh[0:n, j:j + 1]).then_inc(sem("ssh_raw"), 1)
            ac.wait_ge(sem("lgm_ready"), 1)
            e_in = wk[:, 0, :]
            nc.scalar.activation(wk[:, 1, :], e_in, ACT.Exp).then_inc(sem("gexp_ready"), 1)
            ac.wait_ge(sem("route_ready"), 1)
            flag = ac.value_load(flag_i[0:1, 0:1], min_val=0, max_val=1)
            ac.dma_start(gfin, g_final.rearrange("(a n) -> a n", a=1).broadcast_to([P, D])).then_inc(sem("ld_gf"), 16)

            def swiglu_sig(n, k, c):
                ac.wait_ge(sem("gate_ready"), n * 4 + (c + 1))
                nc.scalar.activation(sig[:, c % 2], raw[:, c % 2, 0:2, :], ACT.Sigmoid, scale=ALPHA).then_inc(sem("sig_ready"), 1)

            def y_rows(n, k):
                ac.wait_ge(sem("yT_pe"), n + 1)
                wait(ac, "scattered", n * 16 - 16)
                for half in range(2):
                    nc.scalar.activation(yrow[0:CAP, (k - 1) % 2, half * 512:(half + 1) * 512], banks[4 + half][0:CAP, :],
                                         ACT.Copy, scale=gcol[0:CAP, (k - 1) % UB:(k - 1) % UB + 1]).then_inc(sem("yrow_ready"), 1)

            def expert(n, k):
                swiglu_sig(n, k, 0)
                y_rows(n, k)
                for c in range(1, 4):
                    swiglu_sig(n, k, c)

            for u in range(UB):
                expert(u, u)
            with ac.Fori(1, NE // UB) as it:
                for u in range(UB):
                    expert(it * UB + u, u)
            with ac.If(flag > 0):
                with ac.Fori(0, EXTRA // UB) as it:
                    for u in range(UB):
                        expert(it * UB + (NE + u), u)
            y_rows(flag * EXTRA + NE, 0)
            for j in range(NTT):
                n = ROWS[j]
                ac.wait_ge(sem(f"ld_y{j}"), 16)
                wait(ac, "ssf_raw", j)
                nc.scalar.activation(jf[0:n], yf[0:n, j, :], ACT.Square, accum_out=ssf[0:n, j:j + 1]).then_inc(sem("ssf_raw"), 1)
            ac.wait_ge(sem("st_win"), 32)
            ac.wait_ge(sem("st_out"), 16 * N_OUT_STORES)

        @block.vector
        def _(dv):
            chain = [0]

            def link(ins):
                chain[0] += 1
                ins.then_inc(sem("dve_chain"), 1)
                dv.wait_ge(sem("dve_chain"), chain[0])

            v = nc.vector
            dv.wait_ge(sem("ld_cst"), 16)
            dv.wait_ge(sem("ld_vec"), 16)
            dv.wait_ge(sem("ld_b"), 32)

            def vec(off, n):
                return vecs[:, off:off + n].rearrange("p (k o) -> p k o", o=1)

            def ms(r):
                n = row_tile(r)[1]
                dv.wait_ge(sem("ss_ready"), r + 1)
                v.tensor_scalar(ms7[0:n, r:r + 1], ss7[0:n, r:r + 1], 1.0 / D, EPS, ALU.mult, ALU.add).then_inc(sem("ms_ready"), 1)

            def norm(r):
                ap, n = row_tile(r)
                dv.wait_ge(sem("rs_ready"), r + 1)
                v.tensor_scalar(ap, ap, rs7[0:n, r:r + 1], None, ALU.mult).then_inc(sem("xn_ready"), 1)

            def rows_T(r):
                n = row_tile(r)[1]
                for half in range(2):
                    dv.wait_ge(sem("xT_pe"), 2 * r + half + 1)
                    ks = slice(half * 4, half * 4 + 4)
                    dst = memT[:, ks, r * P:(r + 1) * P] if r < 2 else xT0[:, ks, (r - 2) * P:(r - 2) * P + n]
                    g = vec((G_MEM if r < 2 else G_ATTN) + half * 4, 4).broadcast_to([P, 4, n])
                    src = split(banks[2 * (r % 2) + half][:, :], 4)[:, :, 0:n]
                    v.tensor_tensor(dst, src, g, ALU.mult).then_inc(sem("xT_ready"), 1)

            for r in range(9):
                if r < 7:
                    ms(r)
                if 1 <= r < 8:
                    norm(r - 1)
                if r >= 2:
                    rows_T(r - 2)
            dv.wait_ge(sem("ld_sm"), 48)
            link(v.tensor_tensor(selt, sink[:, 0:8], c_("sel"), ALU.mult))
            link(v.reduce_sum(sink[:, 8:9], selt, axis=AX.X))
            link(v.tensor_copy(sink[:, 9:10], sink[:, 8:9]))
            link(v.tensor_scalar(sink8, sink, 1.0 / SCALE, None, ALU.mult))
            for c in range(2):
                src = vecs[:, STATE:STATE + 32].rearrange("p (b r c) -> p c b r", b=NB, r=2)[:, c]
                v.tensor_copy(us[:, c, :, 0:2], src)

            def z_even(i):
                dv.wait_ge(sem("z_pe"), 2 * i + 1)
                bank = (2 * i) % 8 if 2 * i < NZ1 else 6
                v.tensor_copy(zT[:, Z_ORDER[i], 0:HALF], banks[bank][:, 0:HALF]).then_inc(sem("z_dve"), 1)

            for i in range(len(Z_FIRST)):
                z_even(i)
            for j in (0, 2, 4):
                c0 = P if j < 3 else 0
                dv.wait_ge(sem("kvr_pe"), j + 1)
                v.tensor_copy(kvr[0:ROWS[j], j, c0:256], banks[(NZ1 + j) % 8][0:ROWS[j], c0:256]).then_inc(sem("kvr_dve"), 1)

            def scores(i):
                kind, n, nh, w = UNITS[i]
                s, par = s_view(i), 8 * (i % 2)
                dv.wait_ge(sem("s_pe"), i + 1)
                if i >= 2:
                    dv.wait_ge(sem("job_pe"), JB[i - 1] - 1)
                if kind == "swa":
                    for h in range(nh):
                        slope = 2.0 ** -(h + 1)
                        last = v.scalar_tensor_tensor(out=s[:, h, :], in0=c_("dist")[:, 256 - w:256], scalar=slope / SCALE,
                                                      in1=swa_psum(n, h), op0=ALU.mult, op1=ALU.add)
                    link(last)
                elif kind == "sswa":
                    link(v.tensor_tensor(s, s_psum(i), c_("sbias").rearrange("p (r k) -> p r k", r=2), ALU.add))
                link(v.tensor_reduce(mx[:, 0:nh], s if kind in ("swa", "sswa") else s_psum(i), AX.X, ALU.max))
                if kind in ("swa", "sswa"):
                    sk = slice(0, 8) if kind == "swa" else slice(8, 10)
                    link(v.tensor_tensor(mx[:, 0:nh], mx[:, 0:nh], sink8[:, sk], ALU.max))
                    link(v.tensor_scalar(negm[:, par:par + nh], mx[:, 0:nh], -SCALE, None, ALU.mult))
                    v.tensor_tensor(sarg[:, par:par + nh], negm[:, par:par + nh], sink[:, sk], ALU.add).then_inc(sem("negm_ready"), 1)
                else:
                    v.tensor_scalar(negm[:, par:par + nh], mx[:, 0:nh], -SCALE, None, ALU.mult).then_inc(sem("negm_ready"), 1)

            def denominators(i):
                kind, n, nh, w = UNITS[i]
                a_, b_ = 8 * (i % 2), 8 * (i % 2) + nh
                dv.wait_ge(sem("exp_ready"), i + 1)
                if kind in ("swa", "sswa"):
                    link(v.tensor_tensor(rsum[:, a_:b_], rsum[:, a_:b_], esum[:, a_:b_], ALU.add))
                v.reciprocal(rinv[:, a_:b_], rsum[:, a_:b_]).then_inc(sem("rinv_ready"), 1)

            def conv(c):
                dv.wait_ge(sem("z_act"), len(Z_FIRST) + 2 * c + 2)
                dv.wait_ge(sem("z_dve"), len(Z_FIRST) + 2 * c + 2)
                cc, cv = zT[:, 9 + c, :], zT[:, 11 + c, :]
                link(v.tensor_tensor(cc, cc, cv, ALU.mult))
                w_ = [vecs[:, CONVW + 2 * j + c:CONVW + 2 * j + c + 1] for j in range(3)]
                link(v.tensor_scalar(cv[:, 0:NPR], cc[:, 0:NPR], w_[2], None, ALU.mult))
                link(v.scalar_tensor_tensor(out=cv[:, 1:NPR], in0=cc[:, 0:NPR - 1], scalar=w_[1], in1=cv[:, 1:NPR],
                                            op0=ALU.mult, op1=ALU.add))
                link(v.scalar_tensor_tensor(out=cv[:, 2:NPR], in0=cc[:, 0:NPR - 2], scalar=w_[0], in1=cv[:, 2:NPR],
                                            op0=ALU.mult, op1=ALU.add))
                link(v.tensor_copy(us[:, c, :, 2:6], cc[:, NPR:NT].rearrange("p (b t) -> p b t", b=NB)))
                ys = cv[:, NPR:NT].rearrange("p (b t) -> p b t", b=NB)
                link(v.tensor_scalar(ys, us[:, c, :, 2:6], w_[2], None, ALU.mult))
                link(v.scalar_tensor_tensor(out=ys, in0=us[:, c, :, 1:5], scalar=w_[1], in1=ys, op0=ALU.mult, op1=ALU.add))
                link(v.scalar_tensor_tensor(out=ys, in0=us[:, c, :, 0:4], scalar=w_[0], in1=ys, op0=ALU.mult, op1=ALU.add))

            def conv_gate(c):
                v.tensor_tensor(zT[:, 4 + c, :], zT[:, 4 + c, :], zT[:, 11 + c, :], ALU.mult).then_inc(sem("conv_done"), 1)

            def diagonals():
                dv.wait_ge(sem("z_pe"), 26)
                link(v.memset(qbd, 0.0))
                link(v.memset(mqbd, 0.0))
                for g in range(2):
                    rows = slice(g * HD, (g + 1) * HD)
                    v.tensor_copy(qbd[rows, :, g, :].rearrange("p b (g t) -> p b g t", g=4),
                                  zT[rows, 0:4, NPR:NT].rearrange("p g (b t) -> p b g t", b=NB))
                    v.tensor_copy(mqbd[rows, :, :, g * 4:(g + 1) * 4], zT[rows, 6:8, NPR:NT].rearrange("p c (b t) -> p c b t", b=NB))
                v.tensor_copy(ul[:, :, 0:2], zT[:, 9:11, NPR - 2:NPR])
                v.tensor_copy(ul[:, :, 2:18].rearrange("p c (b r) -> p c b r", b=NB), us[:, :, :, 4:6]).then_inc(sem("diag_ready"), 1)

            zi = len(Z_FIRST)
            scores(0)
            for i in range(NU):
                if i < 4:
                    for _ in Z_LATER[i]:
                        z_even(zi)
                        zi += 1
                denominators(i)
                if i in (0, 1):
                    conv(i)
                if i == 2:
                    dv.wait_ge(sem("z_act"), len(Z_FIRST) + 6)
                    dv.wait_ge(sem("z_dve"), len(Z_FIRST) + 6)
                    conv_gate(0)
                    conv_gate(1)
                if i == 3:
                    dv.wait_ge(sem("z_act"), len(Z_FIRST) + 8)
                    dv.wait_ge(sem("z_dve"), len(Z_FIRST) + 8)
                    diagonals()
                if i == 4:
                    dv.wait_ge(sem("ul_pe"), 1)
                    v.tensor_copy(ulr[0:18], split(banks[7][0:18, 256:512], 2)).then_inc(sem("ulr_ready"), 1)
                if i == 7:
                    dv.wait_ge(sem("st8_pe"), 1)
                    v.tensor_copy(ST, banks[1][:, 0:256]).then_inc(sem("st8_ready"), 1)
                if i == 8:
                    dv.wait_ge(sem("st9_pe"), 1)
                    v.tensor_copy(ST, banks[3][:, 0:256]).then_inc(sem("st9_ready"), 1)
                if i + 1 < NU:
                    scores(i + 1)

            dv.wait_ge(sem("job_out"), JB[NU])
            for t in range(8):
                dv.wait_ge(sem("sq_ready"), t + 1)
                v.tensor_scalar(zT[:, t, :], zT[:, t, :], vecs[:, G_MIX + t:G_MIX + t + 1], None, ALU.mult).then_inc(sem("mix_ready"), 1)
            dv.wait_ge(sem("sq_pe"), NTT)
            ss = banks[6][:, 0:15].rearrange("p (j c) -> p c j", c=3)
            link(v.memset(ss3, 1.0))
            for c, width in ((0, 512), (1, 256), (2, 256)):
                for rows, js in ((P, slice(0, 4)), (NSM, slice(4, 5))):
                    last = v.tensor_scalar(ss3.rearrange("p (j c) -> p c j", c=3)[0:rows, c, js], ss[0:rows, c, js],
                                           1.0 / width, EPS, ALU.mult, ALU.add)
            last.then_inc(sem("ss3_ready"), 1)
            link(v.memset(lg_t[:, :], 0.0))
            dv.wait_ge(sem("rs3_ready"), 1)

            def h_rows(j):
                n, par = ROWS[j], j % 2
                dv.wait_ge(sem(f"ld_xr{par}"), 16 * (j // 2 + 1))
                if j >= 2:
                    dv.wait_ge(sem(f"st_h{par}"), 16 * (j // 2))
                for half in range(2):
                    cols = slice(half * 512, (half + 1) * 512)
                    for part in range(3):
                        dv.wait_ge(sem("h_pe"), j * 6 + half * 3 + part + 1)
                        ins = v.scalar_tensor_tensor(
                            out=hrow[0:n, par, cols], in0=banks[half * 3 + part][0:n, :], scalar=rs3[0:n, j * 3 + part:j * 3 + part + 1],
                            in1=xr[0:n, par, cols] if part == 0 else hrow[0:n, par, cols], op0=ALU.mult, op1=ALU.add)
                        if part < 2:
                            link(ins)
                        else:
                            ins.then_inc(sem("h_ready"), 1)

            def h_norm(j):
                n, par = ROWS[j], j % 2
                if j >= 2:
                    dv.wait_ge(sem(f"st_hn{par}"), 16 * (j // 2))
                dv.wait_ge(sem("ssh_raw"), j + 1)
                v.tensor_scalar(ssh[0:n, j:j + 1], ssh[0:n, j:j + 1], 1.0 / D, EPS, ALU.mult, ALU.add).then_inc(sem("ssh_ready"), 1)
                dv.wait_ge(sem("rsh_ready"), j + 1)
                v.tensor_scalar(hnr[0:n, par, :], hrow[0:n, par, :], rsh[0:n, j:j + 1], None, ALU.mult).then_inc(sem("hn_ready"), 1)

            def h_T(j):
                n, par = ROWS[j], j % 2
                for half in range(2):
                    dv.wait_ge(sem("hT_pe"), 2 * j + half + 1)
                    g = vec(G_FFN + half * 4, 4).broadcast_to([P, 4, n])
                    v.tensor_tensor(hnT[:, par, half * 4:half * 4 + 4, 0:n], split(banks[6 + half][:, :], 4)[:, :, 0:n], g,
                                    ALU.mult).then_inc(sem("hT_ready"), 1)
                dv.wait_ge(sem("lg_pe"), j + 1)
                v.tensor_tensor(lg[0:n, j, :], banks[6][0:n, 0:NE], brt[0:n, :], ALU.add).then_inc(sem("lg_ready"), 1)

            for j in range(NTT):
                h_rows(j)
                if j >= 1:
                    h_T(j - 1)
                h_norm(j)
            h_T(NTT - 1)
            dv.wait_ge(sem("lg_ready"), NTT)
            top = wk[:, 2, 0:40].rearrange("p (j k) -> p j k", j=NTT)
            tid = wk[:, 3, 0:40].bitcast(U32).rearrange("p (j k) -> p j k", j=NTT)
            tidf = wk[:, 4, 0:20].rearrange("p (j k) -> p j k", j=NTT)
            for j in range(NTT):
                last = v.max(top[:, j, :], lg[:, j, :])
            link(last)
            for j in range(NTT):
                last = v.max_index(tid[:, j, :], top[:, j, :], lg[:, j, :])
            link(last)
            link(v.tensor_copy(tidf, tid[:, :, 0:TOPK]))
            m_ = wk[:, 5, :].rearrange("p (j e) -> p j e", j=NTT)

            def b3(ap, shape):
                return ap.broadcast_to(shape)

            hot4 = big1[:, 0:NTT * TOPK * NE].rearrange("p (j k e) -> p j k e", j=NTT, k=TOPK)
            for j in range(NTT):
                for k in range(TOPK):
                    last = v.tensor_scalar(hot4[:, j, k, :], c_("iota"), tidf[:, j, k:k + 1], c_("valid")[:, j:j + 1],
                                           ALU.is_equal, ALU.mult)
            link(last)
            link(v.tensor_reduce(m_, hot4.rearrange("p j k e -> p j e k"), AX.X, ALU.add))
            lm = wk[:, 0, :].rearrange("p (j e) -> p j e", j=NTT)
            v.tensor_tensor(lm, lg, top[:, :, 0:1].broadcast_to([P, NTT, NE]), ALU.subtract).then_inc(sem("lgm_ready"), 1)
            dv.wait_ge(sem("gexp_ready"), 1)
            gx = wk[:, 1, :].rearrange("p (j e) -> p j e", j=NTT)
            link(v.tensor_tensor(gx, gx, m_, ALU.mult))
            gs = wk[:, 6, 0:NTT].rearrange("p (j o) -> p j o", o=1)
            link(v.tensor_reduce(gs, gx, AX.X, ALU.add))
            link(v.tensor_tensor(gs, gs, c_("valid").rearrange("p (j o) -> p j o", o=1), ALU.mult))
            inv = wk[:, 7, 0:NTT].rearrange("p (j o) -> p j o", o=1)
            link(v.tensor_scalar(inv, c_("valid").rearrange("p (j o) -> p j o", o=1), -1.0, 1.0, ALU.mult, ALU.add))
            link(v.tensor_tensor(gs, gs, inv, ALU.add))
            link(v.reciprocal(inv, gs))
            link(v.memset(gate, 0.0))
            link(v.memset(posm, -1.0))
            v.tensor_tensor(gate[:, :, 0:NE], gx, inv.broadcast_to([P, NTT, NE]), ALU.mult).then_inc(sem("m_ready"), 1)
            dv.wait_ge(sem("pos_pe"), 1)
            pos = banks[0][:, 0:160].rearrange("p (j e) -> p j e", j=NTT)
            pt = wk[:, 8, :].rearrange("p (j e) -> p j e", j=NTT)
            link(v.scalar_tensor_tensor(out=pt, in0=pos, scalar=1.0, in1=m_, op0=ALU.add, op1=ALU.mult))
            link(v.tensor_scalar(posm[:, :, 0:NE], pt, -1.0, None, ALU.add))
            link(v.tensor_copy(cnt, banks[0][:, 160:192]))
            link(v.tensor_reduce(wk[:, 9, 0:1], cnt, AX.X, ALU.max))
            link(v.tensor_scalar(wk[:, 9, 1:2], wk[:, 9, 0:1], CAP + 0.5, None, ALU.is_gt))
            link(v.tensor_copy(flag_i[:, :], wk[:, 9, 1:2]))
            flag = dv.value_load(flag_i[0:1, 0:1], min_val=0, max_val=1)

            with dv.If(flag > 0):
                c0 = chain[0]
                nb, ci, cx, t0 = (wk[:, r, 0:NE] for r in (9, 10, 11, 6))
                link(v.tensor_scalar(nb, cnt, CAP + 0.5, None, ALU.is_gt))
                for b in range(2, BLOCKS):
                    link(v.scalar_tensor_tensor(out=nb, in0=cnt, scalar=b * CAP + 0.5, in1=nb, op0=ALU.is_gt, op1=ALU.add))
                src, dst = ci, t0
                link(v.tensor_copy(ci, nb))
                for s in (1, 2, 4, 8, 16):
                    link(v.tensor_copy(dst[:, 0:s], src[:, 0:s]))
                    link(v.tensor_tensor(dst[:, s:NE], src[:, s:NE], src[:, 0:NE - s], ALU.add))
                    src, dst = dst, src
                inc = src
                link(v.tensor_tensor(cx, inc, nb, ALU.subtract))
                sel, tmp, shf = (b[:, 0:EXTRA * NE].rearrange("p (i e) -> p i e", e=NE) for b in (big1, big2, big3))
                for i in range(EXTRA):
                    bi = c_("blk")[:, i:i + 1]
                    link(v.tensor_scalar(tmp[:, i, :], inc, bi, None, ALU.is_gt))
                    link(v.tensor_scalar(sel[:, i, :], cx, bi, None, ALU.is_le))
                    link(v.tensor_scalar(shf[:, i, :], cx, bi, float(-CAP), ALU.subtract, ALU.mult))
                link(v.tensor_tensor(sel, sel, tmp, ALU.mult))
                link(v.tensor_scalar(shf, shf, float(CAP), None, ALU.add))
                one = wk[:, 7, 0:EXTRA]
                link(v.tensor_reduce(one, sel, AX.X, ALU.add))
                link(v.tensor_scalar(one, one, -1.0, None, ALU.add))
                for j in range(NTT):
                    pj, gj = posm[:, j, NE:NE + EXTRA], gate[:, j, NE:NE + EXTRA]
                    pe_ = posm[:, j:j + 1, 0:NE].broadcast_to([P, EXTRA, NE])
                    link(v.tensor_tensor(tmp, pe_, shf, ALU.subtract))
                    link(v.tensor_tensor(tmp, tmp, sel, ALU.mult))
                    link(v.tensor_reduce(pj, tmp, AX.X, ALU.add))
                    link(v.tensor_tensor(pj, pj, one, ALU.add))
                    link(v.tensor_tensor(tmp, gate[:, j:j + 1, 0:NE].broadcast_to([P, EXTRA, NE]), sel, ALU.mult))
                    link(v.tensor_reduce(gj, tmp, AX.X, ALU.add))
                for i in range(EXTRA):
                    link(v.tensor_tensor(tmp[:, i, :], sel[:, i, :], c_("iota"), ALU.mult))
                link(v.tensor_reduce(one, tmp, AX.X, ALU.add))
                link(v.tensor_copy(eid_i[:, 0:EXTRA], one))
                skipped = chain[0] - c0
            with dv.Else():
                v.memset(eid_i[:, 0:EXTRA], 0).then_inc(sem("dve_chain"), skipped)
            dv.wait_ge(sem("dve_chain"), chain[0])

            v.memset(yT, 0.0)
            v.memset(gcol, 0.0)
            v.memset(eid_i[:, EXTRA:EXTRA + 1], 0)
            v.memset(xg, 0.0)
            v.tensor_copy(rv[:, 0, :, 0:1], c_("tokid").rearrange("p (j o) -> p j o", o=1))
            v.tensor_copy(rv[:, 1, :, 0:1], c_("tokid").rearrange("p (j o) -> p j o", o=1))
            v.memset(rv[:, :, :, 2:3], 1.0)
            v.tensor_copy(idx_i[:, UB - 1:UB], c_("pad"))
            link(v.memset(yrow, 0.0))
            v.memset(wk2, 0.0).then_inc(sem("route_ready"), 1)

            def hot_slots(n, k):
                wait(dv, "info_pe", n - 1)
                v.tensor_copy(rv[:, k % 2, :, 1:2], gate[:, :, bass.ds(n, 1)])
                v.tensor_tensor(hot[:, k % 2], c_("slot").rearrange("p (o s) -> p o s", o=1).broadcast_to([P, NTT, CAP]),
                                posm[:, :, bass.ds(n, 1)].broadcast_to([P, NTT, CAP]), ALU.is_equal).then_inc(sem("hot_ready"), 1)

            def slot_info(n, k):
                dv.wait_ge(sem("info_pe"), n + 1)
                wait(dv, "scattered", n * 16 - 32)
                info = banks[7][0:CAP, 416:419]
                free, t = wk2[0:CAP, 0:1], wk2[0:CAP, 1:2]
                v.tensor_scalar(free, info[:, 2:3], -1.0, 1.0, ALU.mult, ALU.add).then_inc(sem("in_a"), 1)
                v.tensor_copy(gcol[0:CAP, k % UB:k % UB + 1], info[:, 1:2])
                dv.wait_ge(sem("in_a"), n + 1)
                v.scalar_tensor_tensor(out=t, in0=free, scalar=c_("pad")[0:CAP], in1=info[:, 0:1], op0=ALU.mult, op1=ALU.add).then_inc(sem("in_b"), 1)
                dv.wait_ge(sem("in_b"), n + 1)
                v.tensor_copy(idx_i[0:CAP, k % UB:k % UB + 1], t).then_inc(sem("idx_ready"), 1)

            def x_T(n, k):
                for half in range(2):
                    dv.wait_ge(sem("xg_pe"), n * 2 + (half + 1))
                    g = vec(G_FFN + half * 4, 4).broadcast_to([P, 4, CAP])
                    v.tensor_tensor(xTe[:, k % 2, half * 4:half * 4 + 4, :], split(banks[6 + half][:, 0:4 * CAP], 4), g,
                                    ALU.mult).then_inc(sem("xTe_ready"), 1)

            def swiglu(n, k, e, c):
                m, r = n * 4 + c, raw[:, c % 2]
                dv.wait_ge(sem("gu_pe"), m + 1)
                for s in range(2):
                    bias = bgu[:, s, bass.ds(e * KD + 2 * c, 2)].rearrange("p (f o) -> p f o", o=1).broadcast_to([P, 2, CAP])
                    last = v.tensor_tensor(r[:, 2 * s:2 * s + 2, :], split(banks[c % 2][:, 0:4 * CAP], 4)[:, 2 * s:2 * s + 2, :], bias, ALU.add)
                last.then_inc(sem("sw_a"), 1)
                dv.wait_ge(sem("sw_a"), m + 1)
                v.tensor_scalar(r[:, 0:2, :], r[:, 0:2, :], LIMIT, None, ALU.min).then_inc(sem("gate_ready"), 1)
                v.tensor_scalar(r[:, 2:4, :], r[:, 2:4, :], LIMIT, -LIMIT, ALU.min, ALU.max).then_inc(sem("sw_b"), 1)
                dv.wait_ge(sem("sw_b"), m + 1)
                dv.wait_ge(sem("gate_ready"), m + 1)
                v.scalar_tensor_tensor(out=r[:, 2:4, :], in0=r[:, 2:4, :], scalar=1.0, in1=r[:, 0:2, :],
                                       op0=ALU.add, op1=ALU.mult).then_inc(sem("sw_c"), 1)
                dv.wait_ge(sem("sw_c"), m + 1)
                dv.wait_ge(sem("sig_ready"), m + 1)
                v.tensor_tensor(act[:, k % 2, 2 * c:2 * c + 2, :], r[:, 2:4, :], sig[:, c % 2], ALU.mult).then_inc(sem("act_ready"), 1)

            def y_T(n, k, e):
                for half in range(2):
                    dv.wait_ge(sem("dn_pe"), n * 2 + 2)
                    bias = bd[:, bass.ds(e * KD + 4 * half, 4)].rearrange("p (f o) -> p f o", o=1).broadcast_to([P, 4, CAP])
                    v.tensor_tensor(yT[:, (k + 1) % 2, half * 4:half * 4 + 4, :], split(banks[2 + half][:, 0:4 * CAP], 4), bias,
                                    ALU.add).then_inc(sem("yT_ready"), 1)

            def expert(n, k, e):
                hot_slots(n + 1, k + 1)
                swiglu(n, k, e, 0)
                swiglu(n, k, e, 1)
                slot_info(n + 1, k + 1)
                swiglu(n, k, e, 2)
                swiglu(n, k, e, 3)
                x_T(n + 1, k + 1)
                y_T(n, k, e)

            hot_slots(0, 0)
            slot_info(0, 0)
            x_T(0, 0)
            for u in range(UB):
                expert(u, u, u)
            with dv.Fori(1, NE // UB) as it:
                for u in range(UB):
                    expert(it * UB + u, u, it * UB + u)
            with dv.If(flag > 0):
                with dv.Fori(0, EXTRA // UB) as it:
                    for u in range(UB):
                        e = dv.value_load(eid_i[0:1, bass.ds(it * UB + u, 1)], min_val=0, max_val=NE - 1)
                        expert(it * UB + (NE + u), u, e)
            dv.wait_ge(sem("ld_gf"), 16)
            for j in range(NTT):
                n = ROWS[j]
                dv.wait_ge(sem("ssf_raw"), j + 1)
                v.tensor_scalar(ssf[0:n, j:j + 1], ssf[0:n, j:j + 1], 1.0 / D, EPS, ALU.mult, ALU.add).then_inc(sem("ssf_ready"), 1)
                dv.wait_ge(sem("rsf_ready"), j + 1)
                v.scalar_tensor_tensor(out=yf[0:n, j, :], in0=yf[0:n, j, :], scalar=rsf[0:n, j:j + 1], in1=gfin[0:n],
                                       op0=ALU.mult, op1=ALU.mult).then_inc(sem("yf_ready"), 1)

        @block.tensor
        def _(pe):
            mm, tr = nc.tensor.matmul, nc.tensor.transpose
            pe.wait_ge(sem("ld_cst"), 16)
            for r in range(7):
                ap, n = row_tile(r)
                pe.wait_ge(sem("xn_ready"), r + 1)
                if r >= 2:
                    pe.wait_ge(sem("xT_ready"), 2 * r - 2)
                for half in range(2):
                    for k in range(4):
                        kk = half * 4 + k
                        last = tr(banks[2 * (r % 2) + half][:, k * P:k * P + n], ap[:, kk * P:(kk + 1) * P], ident[0:n, 0:n])
                    last.then_inc(sem("xT_pe"), 1)
            pe.wait_ge(sem("ld_wm"), 16)
            pe.wait_ge(sem("xT_ready"), 4)
            for m in range(2):
                for k in range(KD):
                    last = mm(banks[5 + m][:, :], memT[:, k, m * P:(m + 1) * P], wm[:, k, :], start=(k == 0), stop=(k == KD - 1))
                last.then_inc(sem("mkv_pe"), 1)
            for m in range(2):
                pe.wait_ge(sem("mkv_ready"), m + 1)
                for c in range(2):
                    last = tr(banks[7][:, c * 256 + m * P:c * 256 + (m + 1) * P], mkv[:, m, c * P:(c + 1) * P], ident)
            last.then_inc(sem("mkT_pe"), 1)
            pe.wait_ge(sem("ld_wi"), 16)
            pe.wait_ge(sem("xT_ready"), 14)

            def w_tile(t, k):
                return wi[:, k, WCOL[t]:WCOL[t] + P]

            def z_half(i, half):
                job = 2 * i + half
                bank = job % 8 if job < NZ1 else 6 + half
                if job == 7:
                    pe.wait_ge(sem("mkT_ready"), 1)
                if 8 <= job < NZ1:
                    pe.wait_ge(sem("z_act" if half else "z_dve"), i - 3)
                if job >= NZ1:
                    pe.wait_ge(sem("z_act" if half else "z_dve"), i)
                for k in range(KD):
                    last = mm(banks[bank][:, 0:HALF], w_tile(Z_ORDER[i], k), xT0[:, k, half * HALF:(half + 1) * HALF],
                              start=(k == 0), stop=(k == KD - 1))
                last.then_inc(sem("z_pe"), 1)

            for i in range(len(Z_FIRST)):
                z_half(i, 0)
                z_half(i, 1)
            for j in range(NTT):
                c0 = P if j < 3 else 0
                job = NZ1 + j
                pe.wait_ge(sem("z_act" if job % 2 else "z_dve"), (job - 8) // 2 + 1)
                for k in range(KD):
                    last = mm(banks[job % 8][0:ROWS[j], c0:256], xT0[:, k, j * P:j * P + ROWS[j]],
                              wi[:, k, 512 + c0:768], start=(k == 0), stop=(k == KD - 1))
                last.then_inc(sem("kvr_pe"), 1)
            pe.wait_ge(sem("kvr_act"), 2)
            pe.wait_ge(sem("kvr_dve"), 3)
            pe.wait_ge(sem("z_act"), len(Z_FIRST))
            pe.wait_ge(sem("z_dve"), len(Z_FIRST))

            def scores(i):
                kind, n, nh, w = UNITS[i]
                if kind == "swa":
                    if n > 0:
                        pe.wait_ge(sem("negm_ready"), i)
                    for t in range(4):
                        for g in range(2):
                            rows = slice(g * HD, (g + 1) * HD)
                            last = mm(swa_psum(n, g * 4 + t), zT[rows, t, n * P:(n + 1) * P],
                                      zT[rows, 8, (n + 1) * P - w:(n + 1) * P], start=True, stop=True)
                elif kind == "mem":
                    pe.wait_ge(sem("negm_ready"), 4)
                    pe.wait_ge(sem("z_dve"), len(Z_ORDER))
                    pe.wait_ge(sem("z_act"), len(Z_ORDER))
                    if i >= 6:
                        pe.wait_ge(sem("exp_ready"), i - 1)
                    for h in range(4):
                        rows = slice((h % 2) * HD, (h % 2 + 1) * HD)
                        last = mm(banks[S_BANK[i] + h % 2][:, (h // 2) * 256:(h // 2 + 1) * 256],
                                  zT[rows, 6 + h // 2, n * P:(n + 1) * P], mkT[rows, h // 2, :], start=True, stop=True)
                elif kind == "sswa":
                    pe.wait_ge(sem("st8_ready"), 1)
                    for r in range(2):
                        tr(banks[0][:, r * 160:r * 160 + P], ST[:, r * P:(r + 1) * P], ident)
                        last = mm(banks[0][:, r * 160 + P:(r + 1) * 160], qbd[:, 4 * r:4 * r + 4].rearrange("p b v n -> p (b v n)"),
                                  zT[:, 8, NPR:NT], start=True, stop=True)
                else:
                    pe.wait_ge(sem("st9_ready"), 1)
                    for half in range(2):
                        last = tr(banks[2][:, half * P:(half + 1) * P], ST[:, half * P:(half + 1) * P], ident)
                last.then_inc(sem("s_pe"), 1)

            def job_bank(j):
                if j >= 2:
                    pe.wait_ge(sem("job_out"), j - 1)
                return banks[4 + j % 2]

            def outputs(i):
                kind, n, nh, w = UNITS[i]
                s, j = s_view(i), JB[i]
                pe.wait_ge(sem("p_ready"), i + 1)
                halves = [1] if (kind, n) == ("swa", 0) else [0, 1]
                if kind == "swa":
                    for g in range(2):
                        for half in halves:
                            bank = job_bank(j)
                            off = (half * P) if w == 256 else 0
                            for t in range(4):
                                last = tr(bank[:, t * P:(t + 1) * P], s[:, g * 4 + t, off:off + P], ident)
                            last.then_inc(sem("job_pe"), 1)
                            j += 1
                    bank = job_bank(j)
                    pe.wait_ge(sem("job_out"), j)
                    for g in range(2):
                        for half in halves:
                            last = mm(bank[g * HD:(g + 1) * HD, :], kvr[:, n - 1 + half, P + g * HD:P + (g + 1) * HD],
                                      pT[:, g * 2 + half, :], start=(half == halves[0]), stop=(half == 1))
                elif kind == "mem":
                    for half in halves:
                        bank = job_bank(j)
                        for h in range(4):
                            last = tr(bank[:, h * P:(h + 1) * P], s[:, (h % 2) * 2 + h // 2, half * P:(half + 1) * P], ident)
                        last.then_inc(sem("job_pe"), 1)
                        j += 1
                    bank = job_bank(j)
                    pe.wait_ge(sem("job_out"), j)
                    for h in range(4):
                        for half in halves:
                            last = mm(bank[(h % 2) * HD:(h % 2 + 1) * HD, (h // 2) * P:(h // 2 + 1) * P],
                                      mkv[:, half, 256 + h * HD:256 + (h + 1) * HD], pT[:, half, h * P:(h + 1) * P],
                                      start=(half == 0), stop=(half == 1))
                elif kind == "sswa":
                    bank = job_bank(j)
                    for r in range(2):
                        tr(bank[:, r * P:(r + 1) * P], s[:, r, 0:P], ident)
                        last = tr(bank[0:32, 256 + r * P:256 + (r + 1) * P], s[:, r, P:160], ident)
                    last.then_inc(sem("job_pe"), 1)
                    j += 1
                    bank = job_bank(j)
                    pe.wait_ge(sem("job_out"), j)
                    pe.wait_ge(sem("ld_vc"), 16)
                    for b in range(NB):
                        cols = slice(b * 32, (b + 1) * 32)
                        mm(bank[:, cols], kvr[0:32, 4, P:256], pT[0:32, 1, cols], start=True, stop=False)
                        last = mm(bank[:, cols], vc[:, b, :], pT[:, 0, cols], start=False, stop=True)
                else:
                    bank = job_bank(j)
                    for half in range(2):
                        last = tr(bank[:, half * P:(half + 1) * P], s[:, 0, half * P:(half + 1) * P], ident)
                    last.then_inc(sem("job_pe"), 1)
                    j += 1
                    bank = job_bank(j)
                    pe.wait_ge(sem("job_out"), j)
                    pe.wait_ge(sem("ld_mcv"), 16)
                    for b in range(NB):
                        for c in range(2):
                            col = (b * 2 + c) * 8
                            for half in range(2):
                                last = mm(bank[:, col:col + 8], mcv[:, b, half, c * P:(c + 1) * P],
                                          pT[:, 0, half * P + col:half * P + col + 8], start=(half == 0), stop=(half == 1))
                last.then_inc(sem("job_pe"), 1)

            zi = len(Z_FIRST)
            scores(0)
            for i in range(NU):
                if i < 4:
                    for _ in Z_LATER[i]:
                        z_half(zi, 0)
                        z_half(zi, 1)
                        zi += 1
                if i == 4:
                    pe.wait_ge(sem("z_dve"), len(Z_ORDER))
                    pe.wait_ge(sem("z_act"), len(Z_ORDER))
                    pe.wait_ge(sem("diag_ready"), 1)
                    for c in range(2):
                        last = tr(banks[7][0:18, 256 + c * P:256 + (c + 1) * P], ul[:, c, :], ident)
                    last.then_inc(sem("ul_pe"), 1)
                if i == 7:
                    pe.wait_ge(sem("ld_kc"), 16)
                    pe.wait_ge(sem("exp_ready"), 7)
                    for b in range(NB):
                        last = mm(banks[1][:, b * 32:(b + 1) * 32], kcT[:, b, :], qbd[:, b].rearrange("p v n -> p (v n)"),
                                  start=True, stop=True)
                    last.then_inc(sem("st8_pe"), 1)
                if i == 8:
                    pe.wait_ge(sem("ld_mck"), 16)
                    pe.wait_ge(sem("exp_ready"), 8)
                    for b in range(NB):
                        for c in range(2):
                            for half in range(2):
                                col = half * P + (b * 2 + c) * 8
                                last = mm(banks[3][:, col:col + 8], mckT[:, c, b, half * P:(half + 1) * P],
                                          mqbd[:, c, b, :], start=True, stop=True)
                    last.then_inc(sem("st9_pe"), 1)
                if i + 1 < NU:
                    scores(i + 1)
                outputs(i)
            pe.wait_ge(sem("job_out"), JB[NU])
            pe.wait_ge(sem("sq_ready"), 8)
            for j in range(NTT):
                n = ROWS[j]
                for part, tiles in enumerate(((0, 1, 2, 3), (4, 5), (6, 7))):
                    for t in tiles:
                        last = mm(banks[6][0:n, j * 3 + part:j * 3 + part + 1], sq[:, t, j * P:j * P + n], c_("ones")[:, 0:1],
                                  start=(t == tiles[0]), stop=(t == tiles[-1]))
                last.then_inc(sem("sq_pe"), 1)
            pe.wait_ge(sem("ld_wo"), 16)
            pe.wait_ge(sem("mix_ready"), 8)

            def router(j):
                n, par = ROWS[j], j % 2
                pe.wait_ge(sem("hn_ready"), j + 1)
                if j == 0:
                    pe.wait_ge(sem("ss3_ready"), 1)
                else:
                    pe.wait_ge(sem("lg_ready"), j)
                for half in range(2):
                    for k in range(4):
                        kk = half * 4 + k
                        last = tr(banks[6 + half][:, k * P:k * P + n], hnr[0:n, par, kk * P:(kk + 1) * P], ident[0:n, 0:n])
                    last.then_inc(sem("hT_pe"), 1)
                pe.wait_ge(sem("hT_ready"), 2 * j + 2)
                for k in range(KD):
                    last = mm(banks[6][0:n, 0:NE], hnT[:, par, k, 0:n], wr[:, k, :], start=(k == 0), stop=(k == KD - 1))
                last.then_inc(sem("lg_pe"), 1)

            for j in range(NTT):
                n = ROWS[j]
                for half in range(2):
                    for part, tiles in enumerate(((0, 1, 2, 3), (4, 5), (6, 7))):
                        if j >= 1:
                            pe.wait_ge(sem("h_ready"), 2 * j - 1 + half)
                        for t in tiles:
                            last = mm(banks[half * 3 + part][0:n, :], zT[:, t, j * P:j * P + n], wo[:, t, half * 512:(half + 1) * 512],
                                      start=(t == tiles[0]), stop=(t == tiles[-1]))
                        last.then_inc(sem("h_pe"), 1)
                if j >= 1:
                    router(j - 1)
            router(NTT - 1)
            pe.wait_ge(sem("m_ready"), 1)
            m_ = wk[:, 5, :].rearrange("p (j e) -> p j e", j=NTT)
            for j in range(NTT):
                for i in range(j + 1):
                    mm(banks[0][:, j * NE:(j + 1) * NE], c_("tri") if i == j else c_("ones"), m_[:, i, :], start=(i == 0), stop=(i == j))
            for i in range(NTT):
                last = mm(banks[0][:, 160:192], c_("ones"), m_[:, i, :], start=(i == 0), stop=(i == NTT - 1))
            last.then_inc(sem("pos_pe"), 1)

            pe.wait_ge(sem("route_ready"), 1)
            flag = pe.value_load(flag_i[0:1, 0:1], min_val=0, max_val=1)

            def info(n, k):
                pe.wait_ge(sem("hot_ready"), n + 1)
                wait(pe, "xTe_ready", n * 2)
                for j in range(NTT):
                    last = mm(banks[7][0:CAP, 416:419], hot[:, k % 2, j, :], rv[:, k % 2, j, :], start=(j == 0), stop=(j == NTT - 1))
                last.then_inc(sem("info_pe"), 1)

            def x_rows(n, k):
                pe.wait_ge(sem("gathered"), n * 16 + 16)
                for half in range(2):
                    for q in range(4):
                        kk = half * 4 + q
                        last = tr(banks[6 + half][:, q * CAP:(q + 1) * CAP], xg[0:CAP, k % 2, kk * P:(kk + 1) * P], ident[0:CAP, 0:CAP])
                    last.then_inc(sem("xg_pe"), 1)

            def y_back(n, k):
                wait(pe, "yT_ready", n * 2)
                wait(pe, "yrow_ready", n * 2)
                for half in range(2):
                    for q in range(4):
                        last = tr(banks[4 + half][0:CAP, q * P:(q + 1) * P], yT[:, k % 2, half * 4 + q, :], ident)
                last.then_inc(sem("yT_pe"), 1)

            def arrived(base, u, q):
                pe.wait_ge(sem(f"chunk{chunk_slot(u, q)}"), base * (16 * USES // UB) + 16 * chunk_fill(u, q))

            def expert(base, u):
                n = base + u
                for c in range(4):
                    arrived(base, u, c)
                    if c == 0:
                        pe.wait_ge(sem("xTe_ready"), n * 2 + 2)
                    w = gu_w(chunk_slot(u, c))
                    wait(pe, "sw_a", n * 4 + (c - 1))
                    for s in range(2):
                        for f in range(2):
                            off = (2 * s + f) * CAP
                            for k in range(KD):
                                last = mm(banks[c % 2][:, off:off + CAP], w[:, s, f, k, :],
                                          xTe[:, u % 2, k, :], start=(k == 0), stop=(k == KD - 1))
                    last.then_inc(sem("gu_pe"), 1)
                    if c == 0:
                        y_back(n, u)
                    if c == 1:
                        info(n + 1, u + 1)
                for c in range(2):
                    arrived(base, u, 4 + c)
                    w = dn_w(chunk_slot(u, 4 + c))
                    for f in range(4):
                        if f % 2 == 0:
                            pe.wait_ge(sem("act_ready"), n * 4 + (2 * c + f // 2 + 1))
                        for t in range(KD):
                            last = mm(banks[2 + t // 4][:, (t % 4) * CAP:(t % 4 + 1) * CAP], w[:, f, t * P:(t + 1) * P],
                                      act[:, u % 2, 4 * c + f, :], start=(c == 0 and f == 0 and t % 4 == 0),
                                      stop=(c == 1 and f == 3), skip_group_check=True)
                    last.then_inc(sem("dn_pe"), 1)
                    if c == 0:
                        x_rows(n + 1, u + 1)

            info(0, 0)
            x_rows(0, 0)
            for u in range(UB):
                expert(0, u)
            with pe.Fori(1, NE // UB) as it:
                for u in range(UB):
                    expert(it * UB, u)
            with pe.If(flag > 0):
                with pe.Fori(0, EXTRA // UB) as it:
                    for u in range(UB):
                        expert(it * UB + NE, u)
            y_back(flag * EXTRA + NE, 0)


def laid_out(x):
    cols = lambda a: a.reshape(-1, P).T
    heads = lambda a: a.reshape(2, 4, HD, -1).transpose(1, 0, 2, 3).reshape(512, -1)
    w_in, w_out, g_mix = x["w_in"][0], x["w_out"][0], x["g_mix_out"][0]
    return {
        "x_prompt": x["x_prompt"], "x_sample": x["x_sample"], "mem_prompt": x["mem_prompt"],
        "cache_win_k": x["cache_win_k"], "cache_win_v": x["cache_win_v"],
        "win_kT": x["cache_win_k"][0].transpose(2, 3, 0, 1).reshape(P, NB, WIN),
        "mem_kT": x["cache_mem_k"][0].transpose(2, 3, 0, 1).reshape(2, P, NB, NMEM).transpose(1, 0, 2, 3),
        "cache_mem_v": x["cache_mem_v"],
        "vectors": np.concatenate([cols(x["g_attn_norm"]), cols(x["g_mem_norm"]),
                                   cols(np.concatenate([heads(g_mix[:512, None])[:, 0], g_mix[512:]])),
                                   cols(x["g_ffn_norm"]), cols(x["conv_w"]), cols(x["state_conv"])], axis=1),
        "w_in": np.concatenate([heads(w_in.T[:512]).T, w_in[:, 512:]], axis=1),
        "attn_sinks": x["attn_sinks"], "w_mem_kv": x["w_mem_kv"],
        "w_out": np.concatenate([heads(w_out[:512]), w_out[512:]], axis=0),
        "w_router": x["w_router"], "b_router": x["b_router"],
        "w_gate_up": x["w_gate_up"].reshape(NE, KD, P, 4, 2, P, 2).transpose(0, 3, 2, 6, 4, 1, 5).reshape(NE * 4, P, CHW),
        "biases_up": x["b_gate_up"].reshape(NE * KD, P, 2).transpose(1, 2, 0).reshape(P, 2 * NE * KD),
        "w_down": x["w_down"].reshape(NE, 2, 4, P, D).transpose(0, 1, 3, 2, 4).reshape(NE * 2, P, CHW),
        "biases_down": cols(x["b_down"]), "g_final": x["g_final"],
    }


_OUTS = [(1, NPR, D), (NB, TS, D), (1, 1, WIN, 2, HD), (1, 1, WIN, 2, HD), (1, 1, 2, 256), (1, 1, NMEM, 4, HD),
         (1, 1, NMEM, 4, HD), (1, NB, WIN, 2, HD), (1, NB, WIN, 2, HD), (1, NB, 2, 256)]


def kernel(**inputs):
    import concourse.bacc as bacc
    from concourse.bass_utils import run_bass_kernel_spmd

    nc = bacc.Bacc("TRN2", target_bir_lowering=False, num_devices=1)
    arrays, args = {}, []
    for name, a in laid_out({k: np.asarray(v) for k, v in inputs.items()}).items():
        a = np.ascontiguousarray(a)
        arrays[f"in_{name}"] = a
        args.append(nc.dram_tensor(f"in_{name}", a.shape, mybir.dt.from_np(a.dtype), kind="ExternalInput").ap())
    for i, shape in enumerate(_OUTS):
        args.append(nc.dram_tensor(f"out_{i}", shape, F32, kind="ExternalOutput").ap())
    build(nc, *args)
    r = run_bass_kernel_spmd(nc, [arrays], core_ids=[0])
    return tuple(r.results[0][f"out_{i}"] for i in range(len(_OUTS)))
```

```python
from contextlib import ExitStack

import numpy as np

import concourse.bass as bass
from concourse import mybir

F32 = mybir.dt.float32
F32R = mybir.dt.float32r
I32 = mybir.dt.int32
U32 = mybir.dt.uint32
ALU = mybir.AluOpType
ACT = mybir.ActivationFunctionType
AX = mybir.AxisListType

P = 128
D = 1024
KD = D // P
NPR, NB, TS = 512, 8, 4
NSM = NB * TS
NT = NPR + NSM
NTT = 5
HD = 64
WIN = 128
NMEM = 256
NE, TOPK = 32, 4
LIMIT, ALPHA = 7.0, 1.702
EPS = 1e-5
SCALE = HD ** -0.5
ROWS = [P, P, P, P, NSM]
HALF = NT // 2
BIG = -1e30

CAP = 104
EXTRA = 20
UB = 4
NCH = 6
CHW = 4096
HALVES = 2 * NCH
HW = CHW // 2
LEAD = 3
HBUF = 4
POOL_T = (2, 5, 8, 11)
NBUF = NCH + HBUF // 2
assert NE % UB == 0 and EXTRA % UB == 0 and HALVES % HBUF == 0
BLOCKS = -(-NT // CAP)
assert EXTRA >= (NT * TOPK) // CAP

_C = {}
_n = 0
for _name, _w in (("ident", P), ("tri", P), ("ones", P), ("dist", 256), ("slot", CAP),
                  ("tokid", NTT), ("pad", 1), ("sel", 8), ("valid", NTT), ("iota", NE), ("blk", EXTRA),
                  ("mhalf", 16), ("eye2", NE), ("sbias", 320)):
    _C[_name] = (_n, _n + _w)
    _n += _w
NCONST = _n


def constants():
    c = np.zeros((P, NCONST), np.float32)
    p = np.arange(P)

    def put(name, v):
        c[:, slice(*_C[name])] = v

    put("ident", np.eye(P))
    put("tri", p[:, None] < p[None, :])
    put("ones", 1.0)
    dist = (P + p)[:, None] - np.arange(256)[None, :]
    put("dist", np.where((dist >= 0) & (dist < WIN), -dist, BIG))
    sb = np.zeros((P, 2, 160), np.float32)
    for r in range(2):
        for row in range(P):
            b, head, t = 4 * r + row // 32, (row // 4) % 8, row % 4
            slope = 2.0 ** -(head + 1)
            dc = WIN + t - np.arange(WIN)
            sb[row, r, :WIN] = np.where(dc < WIN, -slope * dc / SCALE, BIG)
            for j in range(NSM):
                ok = j // TS == b and j % TS <= t
                sb[row, r, WIN + j] = -slope * (t - j % TS) / SCALE if ok else BIG
    put("sbias", sb.reshape(P, 320))
    put("slot", np.arange(CAP)[None, :])
    put("tokid", P * np.arange(NTT)[None, :] + p[:, None])
    put("pad", (NT + p)[:, None])
    put("sel", (p[:, None] // 4) % 8 == np.arange(8)[None, :])
    put("valid", np.arange(NTT)[None, :] * P + p[:, None] < NT)
    put("iota", np.arange(NE)[None, :])
    put("eye2", p[:, None] % NE == np.arange(NE)[None, :])
    put("blk", np.arange(EXTRA)[None, :])
    put("mhalf", -0.5)
    return c


def build(nc, x_prompt, x_sample, mem_prompt, cache_win_k, cache_win_v, win_kT, mem_kT, cache_mem_v,
          vectors, w_in, attn_sinks, w_mem_kv, w_out, g_ffn, w_router, b_router, w_gate_up, w_down, biases,
          g_final,
          y_prompt, y_sample, o_wkp, o_wvp, o_convp, o_mkp, o_mvp, o_wks, o_wvs, o_convs):
    ctx = ExitStack()
    with ctx:
        const_dram = nc.inline_tensor(constants(), name="shape_constants")
        const_dram = const_dram.ap() if hasattr(const_dram, "ap") else const_dram
        hn_tbl = nc.dram_tensor("hn_tbl", (NT, D), F32, kind="Internal").ap()
        y_tbl = nc.dram_tensor("y_tbl", (NT + CAP, D), F32, kind="Internal").ap()

        def sb(name, w, dt=F32):
            return ctx.enter_context(nc.sbuf_tensor(name, [P, w], dt))

        sems = {}

        def sem(name):
            if name not in sems:
                sems[name] = ctx.enter_context(nc.semaphore(name))
            return sems[name]

        with nc.sbuf_tensor("ring", [P, NBUF * CHW], F32) as ring:
            pass
        with ExitStack() as over:
            raw_b = [over.enter_context(nc.sbuf_tensor(f"raw{q}", [P, CHW], F32)) for q in range(NCH)]
        low_b = [sb(f"low{q}", CHW, F32R) for q in range(NCH)]
        high_b = [sb(f"high{i}", HW, F32R) for i in range(HBUF)]
        with nc.sbuf_tensor("area", [P, 8192 + 13 * NT], F32) as area:
            pass
        area_r = sb("area_r", 8192 + 13 * NT, F32R)
        cst = sb("cst", _C["sbias"][0])
        vecs = sb("vecs", 62)
        bias_r = sb("bias_r", 3 * D, F32R)
        pick_r = sb("pick_r", 2 * CAP, F32R)
        wr_t = sb("wr", KD * NE)
        brt = sb("brt", NE)
        small = sb("small", 200)
        us_t = sb("us", 2 * NB * 6)
        lg_t = sb("lg", NTT * NE)
        flag_i = sb("flag_i", 1, I32)
        eid_i = sb("eid_i", EXTRA + 1, I32)
        idx_i = sb("idx_i", UB, I32)

        def c_(name, rows=P):
            a, b = _C[name]
            return cst[0:rows, a:b]

        ident = c_("ident")

        def view(t, off, shape):
            n = int(np.prod(shape))
            names = " ".join(f"d{i}" for i in range(len(shape)))
            ap = t[:, off:off + n]
            if len(shape) == 1:
                return ap
            return ap.rearrange(f"p ({names}) -> p {names}", **{f"d{i}": s for i, s in enumerate(shape)})

        xrow = view(area, 0, [NTT, D])
        memrow = view(area, NTT * D, [2, D])
        junk = view(area, 7 * D, [D])
        wo = view(area, 0, [KD, D])
        zT = view(area, 8192, [13, NT])
        memT = view(area, 8192, [KD, NMEM])
        END = NBUF * CHW
        wi_off = END - KD * 1792
        wi = view(ring, wi_off, [KD, 1792])
        xT0 = view(ring, wi_off - KD * NT, [KD, NT])
        wm = view(ring, wi_off - KD * NT - KD * 512, [KD, 512])
        S_OFF = wi_off - KD * NT - 6144
        Sb = view(ring, S_OFF, [2, 2048])
        pT = view(ring, S_OFF + 4096, [4, 512])
        o = S_OFF + 6144
        mckT = view(ring, o, [2, NB, 256])
        mcv = view(ring, o + 4096, [NB, 2, 256])
        kcT = view(ring, o + 8192, [NB, P])
        vc = view(ring, o + 9216, [NB, P])
        qbd = view(ring, o + 14080, [NB, 2, 16])
        mqbd = view(ring, o + 14336, [2, NB, 8])
        ST = view(ring, o + 14464, [256])
        ul = view(ring, o + 14720, [2, 18])
        ulr = view(ring, o + 14756, [2, P])
        assert o + 15012 <= END
        sq = view(ring, END - 8 * NT, [8, NT])
        h_off = END - 8 * NT - 8192
        xr = view(ring, h_off, [2, D])
        hrow = view(ring, h_off + 2048, [2, D])
        hnr = view(ring, h_off + 4096, [2, D])
        hnT = view(ring, h_off + 6144, [2, KD, P])
        junk_h = view(ring, 4 * CHW, [D])
        gffn = view(ring, 4 * CHW + D, [D])
        assert h_off >= 4 * CHW + 2 * D
        a = [0]

        def moe_buf(shape):
            v = view(area, a[0], shape)
            a[0] += int(np.prod(shape))
            return v

        xg = moe_buf([2, D])
        xH, xL, aH, aL = (view(area_r, a[0] + i * KD * CAP, [KD, CAP]) for i in range(4))
        a[0] += 4 * KD * CAP
        gt = moe_buf([2, 512])
        sg = moe_buf([2, 512])
        up = moe_buf([2, 512])
        yrow = moe_buf([2, D])
        hot = moe_buf([2, NTT, CAP])
        NVC = NE + EXTRA + 1
        a_route = a[0]
        posm = moe_buf([NTT, NVC])
        gate = moe_buf([NTT, NVC])
        rv = moe_buf([2, NTT, 3])
        gcol = moe_buf([UB])
        cnt = moe_buf([NE])
        ptab = moe_buf([NVC])
        wk2 = moe_buf([2])
        nbig = max(NTT * TOPK, EXTRA) * NE
        big1, big2, big3 = (view(area, 2 * D + i * nbig, [nbig]) for i in range(3))
        wk = view(area, 2 * D + 3 * nbig, [12, NTT * NE])
        R_OFF = NCH * CHW + (HBUF - 1) * HW
        hot4 = view(ring, R_OFF, [NTT, TOPK, NE])
        chosen = view(ring, R_OFF + 640, [NTT + 1, NE])
        lm = view(ring, R_OFF + 832, [NTT, NE])
        top = view(ring, R_OFF + 992, [NTT, 8])
        tid = view(ring, R_OFF + 1032, [NTT * 8]).bitcast(U32).rearrange("p (j k) -> p j k", j=NTT)
        tidf = view(ring, R_OFF + 1072, [NTT, TOPK])
        assert a[0] <= 8192 + 13 * NT, a[0]
        assert 2 * D + 3 * nbig + 12 * NTT * NE <= 8448
        yf = view(ring, 2 * CHW, [NTT, D])
        jf = view(ring, 2 * CHW + NTT * D, [D])
        gfin = view(ring, 2 * CHW + (NTT + 1) * D, [D])

        kvr = view(ring, CHW, [NTT, 256])
        mkT = view(ring, CHW + 1280, [2, 256])
        mkv = view(ring, CHW + 1792, [2, 512])
        sbias = view(ring, CHW + 2816, [2, 160])
        assert CHW + 2816 + 320 <= S_OFF
        bias_raw = view(ring, 0, [3 * D])
        wr = wr_t[:, :].rearrange("p (k e) -> p k e", k=KD)
        us = us_t[:, :].rearrange("p (c b r) -> p c b r", c=2, b=NB)
        lg = lg_t[:, :].rearrange("p (j e) -> p j e", j=NTT)
        ss7, ms7, rs7 = small[:, 0:7], small[:, 8:15], small[:, 16:23]
        sink = small[:, 24:34]
        mx, negm, sarg = small[:, 34:42], small[:, 42:58], small[:, 58:74]
        rsum, esum, rinv = small[:, 74:90], small[:, 90:106], small[:, 106:122]
        ss3, rs3 = small[:, 122:137], small[:, 137:152]
        ssh, rsh = small[:, 152:157], small[:, 157:162]
        ssf, rsf = small[:, 162:167], small[:, 167:172]
        sink8 = small[:, 172:182]
        selt = small[:, 182:190]

        G_ATTN, G_MEM, G_MIX, CONVW, STATE = 0, 8, 16, 24, 30

        psum = ctx.enter_context(nc.psum_tensor("psum", [P, 8 * 512], F32))
        banks = [psum[:, i * 512:(i + 1) * 512] for i in range(8)]

        def wait(eng, name, value):
            if not isinstance(value, int) or value > 0:
                eng.wait_ge(sem(name), value)

        def split(ap, n):
            return ap.rearrange("p (a b) -> p a b", a=n)

        def row_tile(r):
            return (memrow[:, r, :], P) if r < 2 else (xrow[0:ROWS[r - 2], r - 2, :], ROWS[r - 2])

        WCOL = {0: 0, 1: 128, 2: 256, 3: 384, 4: 768, 5: 896, 6: 1536, 7: 1664, 8: 512, 9: 1024, 10: 1152, 11: 1280, 12: 1408}
        Z_FIRST = [8, 0, 1, 2, 3]
        Z_LATER = [[9, 11], [10, 12], [4, 5], [6, 7]]
        Z_ORDER = Z_FIRST + [t for g in Z_LATER for t in g]
        NZ1 = 2 * len(Z_FIRST)
        UNITS = [("swa", n, 8, 256 if n else P) for n in range(4)] + \
                [("mem", n, 4, 256) for n in range(4)] + [("sswa", 0, 2, 160), ("smem", 0, 1, 256)]
        NU = len(UNITS)
        PARTS = ((0, 1, 2, 3), (4, 5), (6, 7))
        NJ = [3] + [5] * 3 + [3] * 4 + [2, 2]
        JB = [sum(NJ[:i]) for i in range(NU + 1)]
        S_BANK = [0, 0, 0, 0, 0, 2, 0, 2, 0, 2]

        def s_view(i):
            kind, n, nh, w = UNITS[i]
            return Sb[:, i % 2, 0:nh * w].rearrange("p (h k) -> p h k", h=nh)

        def s_psum(i):
            kind, n, nh, w = UNITS[i]
            if kind == "mem":
                return psum[:, S_BANK[i] * 512:(S_BANK[i] + 2) * 512].rearrange("p (h k) -> p h k", k=256)
            return banks[S_BANK[i]][:, 0:nh * w].rearrange("p (h k) -> p h k", h=nh)

        def swa_psum(n, h):
            w = 256 if n else P
            return banks[h // 2][:, (h % 2) * 256:(h % 2) * 256 + w]

        block = ctx.enter_context(nc.Block())

        N_OUT_STORES = 4 + 2 + 2 * NB + 2

        def raw_w(t, part=0, parts=1):
            n = HW // parts
            return view(raw_b[t // 2], (t % 2) * HW + part * n, [n])

        def low_w(t, part=0, parts=1):
            n = HW // parts
            return view(low_b[t // 2], (t % 2) * HW + part * n, [n])

        def high_w(t, part=0, parts=1):
            n = HW // parts
            return view(high_b[t % HBUF], part * n, [n])

        @block.sync
        def _(sp):
            sp.dma_start(memrow, mem_prompt[0].rearrange("(m p) d -> p m d", p=P)).then_inc(sem("ld_mem"), 16)
            for j in range(4):
                sp.dma_start(xrow[:, j, :], x_prompt[0, j * P:(j + 1) * P, :]).then_inc(sem(f"ld_x{j}"), 16)
            sp.dma_start(xrow[0:NSM, 4, :], x_sample.rearrange("b t d -> (b t) d")).then_inc(sem("ld_x4"), 16)
            sp.dma_start(wm, w_mem_kv[0].rearrange("(k p) n -> p k n", p=P)).then_inc(sem("ld_wm"), 16)
            for c0, c1 in ((0, 768), (768, 1792)):
                sp.dma_start(wi[:, :, c0:c1], w_in[:, c0:c1].rearrange("(k p) n -> p k n", p=P)).then_inc(sem(f"ld_wi{c0}"), 16)

            def load_chunk(e, q):
                src = w_gate_up[e * 4 + q] if q < 4 else w_down[e * 2 + (q - 4)]
                sp.dma_start(raw_b[q][:, :], src).then_inc(sem(f"chunk{q}"), 16)

            sp.wait_ge(sem("xT_pe"), 14)
            sp.dma_start(wo, w_out.rearrange("(k p) n -> p k n", p=P)).then_inc(sem("ld_wo"), 16)
            sp.wait_ge(sem("mkv_ready"), 2)
            for m in range(2):
                sp.dma_start(o_mkp[0, 0, m * P:(m + 1) * P].rearrange("m h d -> m (h d)"),
                             mkv[:, m, 0:256]).then_inc(sem("st_out"), 16)
                sp.dma_start(o_mvp[0, 0, m * P:(m + 1) * P].rearrange("m h d -> m (h d)"),
                             mkv[:, m, 256:512]).then_inc(sem("st_out"), 16)
            sp.wait_ge(sem("kvr_dve"), 3)
            sp.wait_ge(sem("kvr_act"), 2)
            for dst, off in ((o_wkp, 0), (o_wvp, P)):
                sp.dma_start(dst[0, 0].rearrange("s h d -> s (h d)"), kvr[:, 3, off:off + P]).then_inc(sem("st_out"), 16)
            for b in range(NB):
                for dst, off in ((o_wks, 0), (o_wvs, P)):
                    sp.dma_start(dst[0, b, WIN - TS:WIN].rearrange("s h d -> s (h d)"),
                                 kvr[b * TS:(b + 1) * TS, 4, off:off + P]).then_inc(sem("st_out"), 16)
            sp.wait_ge(sem("z_pe"), 26)
            sp.dma_start(kcT, win_kT).then_inc(sem("ld_kc"), 16)
            sp.dma_start(mckT, mem_kT).then_inc(sem("ld_mck"), 16)
            sp.dma_start(vc, cache_win_v[0].rearrange("b s h d -> s b (h d)")).then_inc(sem("ld_vc"), 16)
            sp.dma_start(mcv, cache_mem_v[0].rearrange("b (m p) h d -> p b m (h d)", p=P)).then_inc(sem("ld_mcv"), 16)
            sp.wait_ge(sem("ulr_ready"), 1)
            sp.dma_start(o_convp[0, 0].rearrange("r (c n) -> r c n", c=2), ulr[0:2]).then_inc(sem("st_out"), 16)
            sp.dma_start(o_convs[0].rearrange("b r (c n) -> (b r) c n", c=2), ulr[2:18]).then_inc(sem("st_out"), 16)
            sp.wait_ge(sem("job_pe"), JB[NU])
            sp.wait_ge(sem("st_out"), 16 * N_OUT_STORES)

            def load_x(j):
                src = x_prompt[0, j * P:(j + 1) * P, :] if j < 4 else x_sample.rearrange("b t d -> (b t) d")
                sp.dma_start(xr[0:ROWS[j], j % 2, :], src).then_inc(sem(f"ld_xr{j % 2}"), 16)

            load_x(0)
            load_x(1)
            sp.wait_ge(sem("bias_low"), 1)
            sp.dma_start(gffn, g_ffn.broadcast_to([P, D])).then_inc(sem("ld_gffn"), 16)
            for q in range(4):
                load_chunk(0, q)
            for j in range(NTT):
                sp.wait_ge(sem("h_ready"), 2 * (j + 1))
                if j + 2 < NTT:
                    load_x(j + 2)
                sp.dma_start(y_tbl[j * P:j * P + ROWS[j], :], hrow[0:ROWS[j], j % 2, :]).then_inc(sem(f"st_h{j % 2}"), 16)
                sp.wait_ge(sem("hn_ready"), j + 1)
                sp.dma_start(hn_tbl[j * P:j * P + ROWS[j], :], hnr[0:ROWS[j], j % 2, :]).then_inc(sem(f"st_hn{j % 2}"), 16)
            sp.wait_ge(sem("lg_pe"), NTT)
            sp.wait_ge(sem("sq_pe"), NTT)
            for par, n in ((0, 3), (1, 2)):
                sp.wait_ge(sem(f"st_h{par}"), 16 * n)
                sp.wait_ge(sem(f"st_hn{par}"), 16 * n)
            for q in range(4, NCH):
                load_chunk(0, q)
            sp.wait_ge(sem("route_ready"), 1)
            flag = sp.value_load(flag_i[0:1, 0:1], min_val=0, max_val=1)

            def refill(n, q, expert):
                sp.wait_ge(sem("w_used"), n * HALVES + (2 * q + 2 - HALVES))
                load_chunk(expert, q)

            for n in range(1, UB):
                for q in range(NCH):
                    refill(n, q, n)
            with sp.Fori(1, NE // UB) as it:
                for u in range(UB):
                    for q in range(NCH):
                        refill(it * UB + u, q, it * UB + u)
            AHEAD = 2
            assert 2 * AHEAD > LEAD
            for q in range(AHEAD):
                e = sp.value_load(eid_i[0:1, 0:1], min_val=0, max_val=NE - 1)
                refill(NE, q, e)
            with sp.If(flag > 0):
                with sp.Fori(0, EXTRA // UB) as it:
                    for u in range(UB):
                        e = sp.value_load(eid_i[0:1, bass.ds(it * UB + u, 1)], min_val=0, max_val=NE - 1)
                        for q in range(AHEAD, NCH):
                            refill(it * UB + (NE + u), q, e)
                        e = sp.value_load(eid_i[0:1, bass.ds(it * UB + (u + 1), 1)], min_val=0, max_val=NE - 1)
                        for q in range(AHEAD):
                            refill(it * UB + (NE + u + 1), q, e)
            last = flag * EXTRA + NE
            sp.wait_ge(sem("scattered"), last * 16)
            for j in range(NTT):
                sp.dma_start(yf[0:ROWS[j], j, :], y_tbl[j * P:j * P + ROWS[j], :]).then_inc(sem(f"ld_y{j}"), 16)
            for j in range(NTT):
                sp.wait_ge(sem("yf_ready"), j + 1)
                dst = y_prompt[0, j * P:(j + 1) * P, :] if j < 4 else y_sample.rearrange("b t d -> (b t) d")
                sp.dma_start(dst, yf[0:ROWS[j], j, :]).then_inc(sem("st_y"), 16)
            sp.wait_ge(sem("st_y"), 16 * NTT)

        @block.gpsimd
        def _(pool):
            pool.wait_ge(sem("ld_cst"), 16)
            mh = c_("mhalf")

            def low_part(n, t):
                pool.wait_ge(sem("w_high"), n * HALVES + (t + 1))
                nc.gpsimd.tensor_tensor(low_w(t, 1, 2), raw_w(t, 1, 2), high_w(t, 1, 2), ALU.subtract).then_inc(sem("w_low_pool"), 1)

            for r in range(7):
                n = row_tile(r)[1]
                pool.wait_ge(sem("ms_ready"), r + 1)
                nc.gpsimd.tensor_tensor(rs7[0:n, r:r + 1], ms7[0:n, r:r + 1], mh[0:n, 0:1], ALU.pow).then_inc(sem("rs_ready"), 1)
            for i, (kind, n, nh, w) in enumerate(UNITS):
                s = s_view(i)
                pool.wait_ge(sem("rinv_ready"), i + 1)
                ri = rinv[:, 8 * (i % 2):8 * (i % 2) + nh].rearrange("p (h o) -> p h o", o=1).broadcast_to([P, nh, w])
                nc.gpsimd.tensor_tensor(s, s, ri, ALU.mult).then_inc(sem("p_ready"), 1)
            pool.wait_ge(sem("ss3_ready"), 1)
            nc.gpsimd.tensor_tensor(rs3, ss3, mh[:, 0:15], ALU.pow).then_inc(sem("rs3_ready"), 1)
            for j in range(NTT):
                pool.wait_ge(sem("ssh_ready"), j + 1)
                nc.gpsimd.tensor_tensor(rsh[0:ROWS[j], j:j + 1], ssh[0:ROWS[j], j:j + 1], mh[0:ROWS[j], 0:1],
                                        ALU.pow).then_inc(sem("rsh_ready"), 1)
            pool.wait_ge(sem("lg_pe"), NTT)
            nc.gpsimd.memset(xg, 0.0).then_inc(sem("zeroed"), 1)
            nc.gpsimd.memset(yrow[:, 1, :], 0.0).then_inc(sem("zeroed"), 1)
            pool.wait_ge(sem("zeroed"), 2)
            pool.dma_start(y_tbl[NT:NT + CAP, :], yrow[0:CAP, 1, :]).then_inc(sem("pad_rows"), 16)
            pool.wait_ge(sem("route_ready"), 1)
            for par, n in ((0, 3), (1, 2)):
                pool.wait_ge(sem(f"st_hn{par}"), 16 * n)

            bound = pool.alloc_register("bound")
            none = pool.value_load(eid_i[0:1, EXTRA:EXTRA + 1], min_val=0, max_val=0)

            def gather(n, k):
                pool.wait_ge(sem("idx_ready"), n + 1)
                pool.reg_add(bound, none, NT - 1)
                nc.gpsimd.indirect_dma_start(
                    xg[0:CAP, k % 2, :], None, hn_tbl[:, :],
                    bass.IndirectOffsetOnAxis(ap=idx_i[0:CAP, k % UB:k % UB + 1].bitcast(U32), axis=0),
                    bounds_check=bound, oob_is_err=False).then_inc(sem("gathered"), 16)

            def scatter(n, k):
                pool.wait_ge(sem("yrow_ready"), n * 2)
                wait(pool, "scattered", n * 16 - 16)
                pool.reg_add(bound, none, NT + CAP - 1)
                nc.gpsimd.indirect_dma_start(
                    y_tbl[:, :], bass.IndirectOffsetOnAxis(ap=idx_i[0:CAP, (k - 1) % UB:(k - 1) % UB + 1].bitcast(U32), axis=0),
                    yrow[0:CAP, (k - 1) % 2, :], None,
                    bounds_check=bound, oob_is_err=True, compute_op=ALU.add).then_inc(sem("scattered"), 16)

            flag = pool.value_load(flag_i[0:1, 0:1], min_val=0, max_val=1)

            def expert(n, k):
                if not isinstance(n, int) or n > 0:
                    scatter(n, k)
                low_part(n, 5)
                gather(n + 1, k + 1)
                low_part(n, 8)
                low_part(n, 11)
                low_part(n + 1, 2)

            gather(0, 0)
            low_part(0, 2)
            pool.wait_ge(sem("pad_rows"), 16)
            for par, n in ((0, 3), (1, 2)):
                pool.wait_ge(sem(f"st_h{par}"), 16 * n)
            for u in range(UB):
                expert(u, u)
            with pool.Fori(1, NE // UB) as it:
                for u in range(UB):
                    expert(it * UB + u, u)
            with pool.If(flag > 0):
                with pool.Fori(0, EXTRA // UB) as it:
                    for u in range(UB):
                        expert(it * UB + (NE + u), u)
            last = flag * EXTRA + NE
            scatter(last, 0)
            for j in range(NTT):
                pool.wait_ge(sem("ssf_ready"), j + 1)
                nc.gpsimd.tensor_tensor(rsf[0:ROWS[j], j:j + 1], ssf[0:ROWS[j], j:j + 1], mh[0:ROWS[j], 0:1],
                                        ALU.pow).then_inc(sem("rsf_ready"), 1)

        @block.scalar
        def _(ac):
            ac.dma_start(cst[:, :], const_dram[:, 0:_C["sbias"][0]]).then_inc(sem("ld_cst"), 16)
            ac.dma_start(vecs[:, :], vectors).then_inc(sem("ld_vec"), 16)
            for r in range(7):
                ap, n = row_tile(r)
                if r == 0:
                    ac.wait_ge(sem("ld_mem"), 16)
                elif r >= 2:
                    ac.wait_ge(sem(f"ld_x{r - 2}"), 16)
                wait(ac, "ss_ready", r)
                nc.scalar.activation(junk[0:n], ap, ACT.Square, accum_out=ss7[0:n, r:r + 1]).then_inc(sem("ss_ready"), 1)
            ac.dma_start(sink[:, 0:8], attn_sinks[0:1, :].broadcast_to([P, 8])).then_inc(sem("ld_sm"), 16)
            ac.dma_start(brt[:, :], b_router[0:1, :].broadcast_to([P, NE])).then_inc(sem("ld_sm"), 16)
            ac.dma_start(wr, w_router[0].rearrange("(k p) e -> p k e", p=P)).then_inc(sem("ld_sm"), 16)
            for g in range(2):
                ac.dma_start(bias_raw[g * NE:(g + 1) * NE], biases).then_inc(sem("ld_b"), 16)
            ac.dma_start(sbias, const_dram[:, _C["sbias"][0]:NCONST].rearrange("p (r k) -> p r k", r=2)).then_inc(sem("ld_sb"), 16)
            for dst, src in ((o_wks, cache_win_k), (o_wvs, cache_win_v)):
                ac.dma_start(dst[0, :, 0:WIN - TS].rearrange("b s h d -> b (s h d)"),
                             src[0, :, TS:WIN].rearrange("b s h d -> b (s h d)")).then_inc(sem("st_win"), 16)
            for m in range(2):
                ac.wait_ge(sem("mkv_pe"), m + 1)
                nc.scalar.copy(mkv[:, m, :], banks[5 + m][:, :]).then_inc(sem("mkv_ready"), 1)
            ac.wait_ge(sem("mkT_pe"), 1)
            nc.scalar.copy(view(ring, CHW + 1280, [512]), banks[7][:, :]).then_inc(sem("mkT_ready"), 1)

            def z_odd(i):
                ac.wait_ge(sem("z_pe"), 2 * i + 2)
                bank = (2 * i + 1) % 8 if 2 * i < NZ1 else 7
                nc.scalar.copy(zT[:, Z_ORDER[i], HALF:NT], banks[bank][:, 0:HALF]).then_inc(sem("z_act"), 1)

            for i in range(len(Z_FIRST)):
                z_odd(i)
            for j in (1, 3):
                c0 = P if j < 3 else 0
                ac.wait_ge(sem("kvr_pe"), j + 1)
                nc.scalar.copy(kvr[0:ROWS[j], j, c0:256], banks[(NZ1 + j) % 8][0:ROWS[j], c0:256]).then_inc(sem("kvr_act"), 1)

            def softmax_exp(i):
                kind, n, nh, w = UNITS[i]
                s, par = s_view(i), 8 * (i % 2)
                ac.wait_ge(sem("negm_ready"), i + 1)
                if kind in ("mem", "smem"):
                    ac.wait_ge(sem("job_pe"), JB[i - 1] - 1)
                if kind in ("swa", "sswa"):
                    nc.scalar.activation(esum[:, par:par + nh], sarg[:, par:par + nh], ACT.Exp)
                for h in range(nh):
                    src = s_psum(i)[:, h, :] if kind in ("mem", "smem") else s[:, h, :]
                    last = nc.scalar.activation(s[:, h, :], src, ACT.Exp, bias=negm[:, par + h:par + h + 1], scale=SCALE,
                                                accum_out=rsum[:, par + h:par + h + 1])
                last.then_inc(sem("exp_ready"), 1)

            def move_out(i):
                kind, n, nh, w = UNITS[i]
                for k in range(NJ[i] - 1):
                    ac.wait_ge(sem("job_pe"), JB[i] + k + 1)
                    bank = banks[4 + (JB[i] + k) % 2]
                    if kind == "swa":
                        g, half = (k, 1) if n == 0 else (k // 2, k % 2)
                        nc.scalar.copy(pT[:, g * 2 + half, :], bank[:, :]).then_inc(sem("job_out"), 1)
                    elif kind == "mem":
                        nc.scalar.copy(pT[:, k, :], bank[:, :]).then_inc(sem("job_out"), 1)
                    elif kind == "sswa":
                        nc.scalar.copy(pT[:, 0, 0:256], bank[:, 0:256])
                        nc.scalar.copy(pT[0:32, 1, 0:256], bank[0:32, 256:512]).then_inc(sem("job_out"), 1)
                    else:
                        nc.scalar.copy(pT[:, 0, 0:256], bank[:, 0:256]).then_inc(sem("job_out"), 1)
                if i < NU - 1:
                    softmax_exp(i + 1)
                k = JB[i + 1] - 1
                ac.wait_ge(sem("job_pe"), k + 1)
                bank = banks[4 + k % 2]
                if kind == "swa":
                    nc.scalar.copy(zT[:, 0:4, n * P:(n + 1) * P], split(bank[:, :], 4)).then_inc(sem("job_out"), 1)
                elif kind == "mem":
                    nc.scalar.copy(zT[:, 6:8, n * P:(n + 1) * P], split(bank[:, 0:256], 2)).then_inc(sem("job_out"), 1)
                elif kind == "sswa":
                    for g in range(2):
                        rows = slice(g * HD, (g + 1) * HD)
                        src = bank[rows, 0:256].rearrange("p (b v g t) -> p v b g t", b=NB, v=2, g=4)[:, g]
                        dst = zT[rows, 0:4, NPR:NT].rearrange("p g (b t) -> p b g t", b=NB)
                        last = nc.scalar.copy(dst, src)
                    last.then_inc(sem("job_out"), 1)
                else:
                    for g in range(2):
                        rows = slice(g * HD, (g + 1) * HD)
                        src = bank[rows, 0:P].rearrange("p (b c v t) -> p v b c t", b=NB, c=2, v=2)[:, g]
                        dst = zT[rows, 6:8, NPR:NT].rearrange("p c (b t) -> p b c t", b=NB)
                        last = nc.scalar.copy(dst, src)
                    last.then_inc(sem("job_out"), 1)

            zi = len(Z_FIRST)
            softmax_exp(0)
            for i in range(NU):
                if i < 4:
                    for _ in Z_LATER[i]:
                        z_odd(zi)
                        zi += 1
                move_out(i)
                if i == 4:
                    ac.wait_ge(sem("ld_b"), 32)
                    nc.scalar.copy(bias_r[0:2 * NE, :], bias_raw[0:2 * NE]).then_inc(sem("bias_high"), 1)

            ac.wait_ge(sem("conv_done"), 2)
            ac.wait_ge(sem("job_out"), JB[NU])
            ac.wait_ge(sem("st_out"), 16 * N_OUT_STORES)
            for t in range(8):
                nc.scalar.activation(sq[:, t, :], zT[:, t, :], ACT.Square).then_inc(sem("sq_ready"), 1)
            def h_T(j):
                n = ROWS[j]
                for half in range(2):
                    ac.wait_ge(sem("hT_pe"), 2 * j + half + 1)
                    nc.scalar.copy(hnT[:, j % 2, half * 4:half * 4 + 4, 0:n],
                                   split(banks[6 + half][:, :], 4)[:, :, 0:n]).then_inc(sem("hT_ready"), 1)

            for j in range(NTT):
                n = ROWS[j]
                if j >= 1:
                    h_T(j - 1)
                ac.wait_ge(sem("h_ready"), 2 * (j + 1))
                wait(ac, "ssh_raw", j)
                nc.scalar.activation(junk_h[0:n], hrow[0:n, j % 2, :], ACT.Square, accum_out=ssh[0:n, j:j + 1]).then_inc(sem("ssh_raw"), 1)
            h_T(NTT - 1)
            ac.wait_ge(sem("lgm_ready"), NTT)
            nc.scalar.activation(wk[:, 1, :], lm.rearrange("p j e -> p (j e)"), ACT.Exp).then_inc(sem("gexp_ready"), 1)
            ac.wait_ge(sem("route_ready"), 1)
            flag = ac.value_load(flag_i[0:1, 0:1], min_val=0, max_val=1)

            def high_part(n, t):
                ac.wait_ge(sem(f"chunk{t // 2}"), n * 16 + 16)
                wait(ac, "w_used", n * HALVES + (t - HBUF + 1))
                nc.scalar.copy(high_w(t), raw_w(t)).then_inc(sem("w_high"), 1)

            def y_rows(n, k):
                ac.wait_ge(sem("w_used"), n * HALVES)
                wait(ac, "scattered", n * 16 - 32)
                for half in range(2):
                    nc.scalar.activation(yrow[0:CAP, (k - 1) % 2, half * 512:(half + 1) * 512], banks[4 + half][0:CAP, :],
                                         ACT.Copy, scale=gcol[0:CAP, (k - 1) % UB:(k - 1) % UB + 1]).then_inc(sem("yrow_ready"), 1)

            def gate_sigmoid(n, fh):
                ac.wait_ge(sem("gate_ready"), n * 2 + (fh + 1))
                wait(ac, "act_ready", n * 2 + (fh - 1))
                nc.scalar.activation(sg[0:CAP, fh, :], gt[0:CAP, fh, :], ACT.Sigmoid, scale=ALPHA).then_inc(sem("sig_ready"), 1)

            def act_high(n, fh):
                ac.wait_ge(sem("act_pe"), n * 2 + (fh + 1))
                nc.scalar.copy(aH[:, 4 * fh:4 * fh + 4, :], split(banks[6 + fh][:, 0:4 * CAP], 4)).then_inc(sem("act_high"), 1)

            def x_high(n):
                for half in range(2):
                    ac.wait_ge(sem("xg_pe"), n * 2 + (half + 1))
                    nc.scalar.copy(xH[:, 4 * half:4 * half + 4, :], split(banks[half][:, 0:4 * CAP], 4)).then_inc(sem("x_high"), 1)

            def expert(n, k):
                for t in range(HALVES):
                    if t == 0 and (not isinstance(n, int) or n > 0):
                        y_rows(n, k)
                    if t in (4, 8):
                        gate_sigmoid(n, (t - 4) // 4)
                    if t in (6, 10):
                        act_high(n, (t - 6) // 4)
                    if t == 10:
                        x_high(n + 1)
                    high_part(n + (t + LEAD) // HALVES, (t + LEAD) % HALVES)

            ac.wait_ge(sem("lg_pe"), NTT)
            ac.wait_ge(sem("sq_pe"), NTT)
            for par, n in ((0, 3), (1, 2)):
                ac.wait_ge(sem(f"st_h{par}"), 16 * n)
                ac.wait_ge(sem(f"st_hn{par}"), 16 * n)
            for t in range(LEAD):
                high_part(0, t)
            x_high(0)
            for u in range(UB):
                expert(u, u)
            with ac.Fori(1, NE // UB) as it:
                for u in range(UB):
                    expert(it * UB + u, u)
            with ac.If(flag > 0):
                with ac.Fori(0, EXTRA // UB) as it:
                    for u in range(UB):
                        expert(it * UB + (NE + u), u)
            y_rows(flag * EXTRA + NE, 0)
            ac.dma_start(gfin, g_final.rearrange("(a n) -> a n", a=1).broadcast_to([P, D])).then_inc(sem("ld_gf"), 16)
            for j in range(NTT):
                n = ROWS[j]
                ac.wait_ge(sem(f"ld_y{j}"), 16)
                wait(ac, "ssf_raw", j)
                nc.scalar.activation(jf[0:n], yf[0:n, j, :], ACT.Square, accum_out=ssf[0:n, j:j + 1]).then_inc(sem("ssf_raw"), 1)
            ac.wait_ge(sem("st_win"), 32)
            ac.wait_ge(sem("st_out"), 16 * N_OUT_STORES)

        @block.vector
        def _(dv):
            chain = [0]

            def link(ins):
                chain[0] += 1
                ins.then_inc(sem("dve_chain"), 1)
                dv.wait_ge(sem("dve_chain"), chain[0])

            v = nc.vector
            dv.wait_ge(sem("ld_cst"), 16)
            dv.wait_ge(sem("ld_vec"), 16)

            def vec(off, n):
                return vecs[:, off:off + n].rearrange("p (k o) -> p k o", o=1)

            def ms(r):
                n = row_tile(r)[1]
                dv.wait_ge(sem("ss_ready"), r + 1)
                v.tensor_scalar(ms7[0:n, r:r + 1], ss7[0:n, r:r + 1], 1.0 / D, EPS, ALU.mult, ALU.add).then_inc(sem("ms_ready"), 1)

            def norm(r):
                ap, n = row_tile(r)
                dv.wait_ge(sem("rs_ready"), r + 1)
                v.tensor_scalar(ap, ap, rs7[0:n, r:r + 1], None, ALU.mult).then_inc(sem("xn_ready"), 1)

            def rows_T(r):
                n = row_tile(r)[1]
                for half in range(2):
                    dv.wait_ge(sem("xT_pe"), 2 * r + half + 1)
                    ks = slice(half * 4, half * 4 + 4)
                    dst = memT[:, ks, r * P:(r + 1) * P] if r < 2 else xT0[:, ks, (r - 2) * P:(r - 2) * P + n]
                    g = vec((G_MEM if r < 2 else G_ATTN) + half * 4, 4).broadcast_to([P, 4, n])
                    src = split(banks[2 * (r % 2) + half][:, :], 4)[:, :, 0:n]
                    v.tensor_tensor(dst, src, g, ALU.mult).then_inc(sem("xT_ready"), 1)

            for r in range(9):
                if r < 7:
                    ms(r)
                if 1 <= r < 8:
                    norm(r - 1)
                if r >= 2:
                    rows_T(r - 2)
            dv.wait_ge(sem("ld_sm"), 48)
            link(v.tensor_tensor(selt, sink[:, 0:8], c_("sel"), ALU.mult))
            link(v.reduce_sum(sink[:, 8:9], selt, axis=AX.X))
            link(v.tensor_copy(sink[:, 9:10], sink[:, 8:9]))
            link(v.tensor_scalar(sink8, sink, 1.0 / SCALE, None, ALU.mult))
            for c in range(2):
                src = vecs[:, STATE:STATE + 32].rearrange("p (b r c) -> p c b r", b=NB, r=2)[:, c]
                v.tensor_copy(us[:, c, :, 0:2], src)

            def z_even(i):
                dv.wait_ge(sem("z_pe"), 2 * i + 1)
                bank = (2 * i) % 8 if 2 * i < NZ1 else 6
                v.tensor_copy(zT[:, Z_ORDER[i], 0:HALF], banks[bank][:, 0:HALF]).then_inc(sem("z_dve"), 1)

            for i in range(len(Z_FIRST)):
                z_even(i)
            for j in (0, 2, 4):
                c0 = P if j < 3 else 0
                dv.wait_ge(sem("kvr_pe"), j + 1)
                v.tensor_copy(kvr[0:ROWS[j], j, c0:256], banks[(NZ1 + j) % 8][0:ROWS[j], c0:256]).then_inc(sem("kvr_dve"), 1)

            def scores(i):
                kind, n, nh, w = UNITS[i]
                s, par = s_view(i), 8 * (i % 2)
                dv.wait_ge(sem("s_pe"), i + 1)
                if i >= 2:
                    dv.wait_ge(sem("job_pe"), JB[i - 1] - 1)
                if kind == "swa":
                    for h in range(nh):
                        slope = 2.0 ** -(h + 1)
                        last = v.scalar_tensor_tensor(out=s[:, h, :], in0=c_("dist")[:, 256 - w:256], scalar=slope / SCALE,
                                                      in1=swa_psum(n, h), op0=ALU.mult, op1=ALU.add)
                    link(last)
                elif kind == "sswa":
                    dv.wait_ge(sem("ld_sb"), 16)
                    link(v.tensor_tensor(s, s_psum(i), sbias, ALU.add))
                link(v.tensor_reduce(mx[:, 0:nh], s if kind in ("swa", "sswa") else s_psum(i), AX.X, ALU.max))
                if kind in ("swa", "sswa"):
                    sk = slice(0, 8) if kind == "swa" else slice(8, 10)
                    link(v.tensor_tensor(mx[:, 0:nh], mx[:, 0:nh], sink8[:, sk], ALU.max))
                    link(v.tensor_scalar(negm[:, par:par + nh], mx[:, 0:nh], -SCALE, None, ALU.mult))
                    v.tensor_tensor(sarg[:, par:par + nh], negm[:, par:par + nh], sink[:, sk], ALU.add).then_inc(sem("negm_ready"), 1)
                else:
                    v.tensor_scalar(negm[:, par:par + nh], mx[:, 0:nh], -SCALE, None, ALU.mult).then_inc(sem("negm_ready"), 1)

            def denominators(i):
                kind, n, nh, w = UNITS[i]
                a_, b_ = 8 * (i % 2), 8 * (i % 2) + nh
                dv.wait_ge(sem("exp_ready"), i + 1)
                if kind in ("swa", "sswa"):
                    link(v.tensor_tensor(rsum[:, a_:b_], rsum[:, a_:b_], esum[:, a_:b_], ALU.add))
                v.reciprocal(rinv[:, a_:b_], rsum[:, a_:b_]).then_inc(sem("rinv_ready"), 1)

            def conv(c):
                dv.wait_ge(sem("z_act"), len(Z_FIRST) + 2 * c + 2)
                dv.wait_ge(sem("z_dve"), len(Z_FIRST) + 2 * c + 2)
                cc, cv = zT[:, 9 + c, :], zT[:, 11 + c, :]
                link(v.tensor_tensor(cc, cc, cv, ALU.mult))
                w_ = [vecs[:, CONVW + 2 * j + c:CONVW + 2 * j + c + 1] for j in range(3)]
                link(v.tensor_scalar(cv[:, 0:NPR], cc[:, 0:NPR], w_[2], None, ALU.mult))
                link(v.scalar_tensor_tensor(out=cv[:, 1:NPR], in0=cc[:, 0:NPR - 1], scalar=w_[1], in1=cv[:, 1:NPR],
                                            op0=ALU.mult, op1=ALU.add))
                link(v.scalar_tensor_tensor(out=cv[:, 2:NPR], in0=cc[:, 0:NPR - 2], scalar=w_[0], in1=cv[:, 2:NPR],
                                            op0=ALU.mult, op1=ALU.add))
                link(v.tensor_copy(us[:, c, :, 2:6], cc[:, NPR:NT].rearrange("p (b t) -> p b t", b=NB)))
                ys = cv[:, NPR:NT].rearrange("p (b t) -> p b t", b=NB)
                link(v.tensor_scalar(ys, us[:, c, :, 2:6], w_[2], None, ALU.mult))
                link(v.scalar_tensor_tensor(out=ys, in0=us[:, c, :, 1:5], scalar=w_[1], in1=ys, op0=ALU.mult, op1=ALU.add))
                link(v.scalar_tensor_tensor(out=ys, in0=us[:, c, :, 0:4], scalar=w_[0], in1=ys, op0=ALU.mult, op1=ALU.add))

            def conv_gate(c):
                v.tensor_tensor(zT[:, 4 + c, :], zT[:, 4 + c, :], zT[:, 11 + c, :], ALU.mult).then_inc(sem("conv_done"), 1)

            def diagonals():
                dv.wait_ge(sem("z_pe"), 26)
                link(v.memset(qbd, 0.0))
                link(v.memset(mqbd, 0.0))
                for g in range(2):
                    rows = slice(g * HD, (g + 1) * HD)
                    v.tensor_copy(qbd[rows, :, g, :].rearrange("p b (g t) -> p b g t", g=4),
                                  zT[rows, 0:4, NPR:NT].rearrange("p g (b t) -> p b g t", b=NB))
                    v.tensor_copy(mqbd[rows, :, :, g * 4:(g + 1) * 4], zT[rows, 6:8, NPR:NT].rearrange("p c (b t) -> p c b t", b=NB))
                v.tensor_copy(ul[:, :, 0:2], zT[:, 9:11, NPR - 2:NPR])
                v.tensor_copy(ul[:, :, 2:18].rearrange("p c (b r) -> p c b r", b=NB), us[:, :, :, 4:6]).then_inc(sem("diag_ready"), 1)

            zi = len(Z_FIRST)
            scores(0)
            for i in range(NU):
                if i < 4:
                    for _ in Z_LATER[i]:
                        z_even(zi)
                        zi += 1
                denominators(i)
                if i in (0, 1):
                    conv(i)
                if i == 2:
                    dv.wait_ge(sem("z_act"), len(Z_FIRST) + 6)
                    dv.wait_ge(sem("z_dve"), len(Z_FIRST) + 6)
                    conv_gate(0)
                    conv_gate(1)
                if i == 3:
                    dv.wait_ge(sem("z_act"), len(Z_FIRST) + 8)
                    dv.wait_ge(sem("z_dve"), len(Z_FIRST) + 8)
                    diagonals()
                if i == 4:
                    dv.wait_ge(sem("ul_pe"), 1)
                    v.tensor_copy(ulr[0:18], split(banks[7][0:18, 256:512], 2)).then_inc(sem("ulr_ready"), 1)
                if i == 7:
                    dv.wait_ge(sem("bias_high"), 1)
                    v.tensor_tensor(bias_r[NE:2 * NE, :], bias_raw[NE:2 * NE], bias_r[NE:2 * NE, :], ALU.subtract).then_inc(sem("bias_low"), 1)
                    dv.wait_ge(sem("st8_pe"), 1)
                    v.tensor_copy(ST, banks[1][:, 0:256]).then_inc(sem("st8_ready"), 1)
                if i == 8:
                    dv.wait_ge(sem("st9_pe"), 1)
                    v.tensor_copy(ST, banks[3][:, 0:256]).then_inc(sem("st9_ready"), 1)
                if i + 1 < NU:
                    scores(i + 1)

            dv.wait_ge(sem("job_out"), JB[NU])
            for t in range(8):
                dv.wait_ge(sem("sq_ready"), t + 1)
                v.tensor_scalar(zT[:, t, :], zT[:, t, :], vecs[:, G_MIX + t:G_MIX + t + 1], None, ALU.mult).then_inc(sem("mix_ready"), 1)
            adds = [(tiles[0], t) for tiles in PARTS for t in tiles[1:]]
            for first, t in adds:
                ins = v.tensor_tensor(sq[:, first, :], sq[:, first, :], sq[:, t, :], ALU.add)
                if (first, t) == adds[-1]:
                    ins.then_inc(sem("sq_sums"), 1)
                else:
                    link(ins)
            dv.wait_ge(sem("sq_pe"), NTT)
            ss = banks[6][:, 0:15].rearrange("p (j c) -> p c j", c=3)
            link(v.memset(ss3, 1.0))
            for c, width in ((0, 512), (1, 256), (2, 256)):
                for rows, js in ((P, slice(0, 4)), (NSM, slice(4, 5))):
                    last = v.tensor_scalar(ss3.rearrange("p (j c) -> p c j", c=3)[0:rows, c, js], ss[0:rows, c, js],
                                           1.0 / width, EPS, ALU.mult, ALU.add)
            last.then_inc(sem("ss3_ready"), 1)
            link(v.memset(lg_t[:, :], 0.0))
            dv.wait_ge(sem("rs3_ready"), 1)

            def h_rows(j):
                n, par = ROWS[j], j % 2
                dv.wait_ge(sem(f"ld_xr{par}"), 16 * (j // 2 + 1))
                if j >= 2:
                    dv.wait_ge(sem(f"st_h{par}"), 16 * (j // 2))
                for half in range(2):
                    cols = slice(half * 512, (half + 1) * 512)
                    for part in range(3):
                        dv.wait_ge(sem("h_pe"), j * 6 + half * 3 + part + 1)
                        ins = v.scalar_tensor_tensor(
                            out=hrow[0:n, par, cols], in0=banks[half * 3 + part][0:n, :], scalar=rs3[0:n, j * 3 + part:j * 3 + part + 1],
                            in1=xr[0:n, par, cols] if part == 0 else hrow[0:n, par, cols], op0=ALU.mult, op1=ALU.add)
                        if part < 2:
                            link(ins)
                        else:
                            ins.then_inc(sem("h_ready"), 1)

            def h_norm(j):
                n, par = ROWS[j], j % 2
                if j >= 2:
                    dv.wait_ge(sem(f"st_hn{par}"), 16 * (j // 2))
                dv.wait_ge(sem("ssh_raw"), j + 1)
                v.tensor_scalar(ssh[0:n, j:j + 1], ssh[0:n, j:j + 1], 1.0 / D, EPS, ALU.mult, ALU.add).then_inc(sem("ssh_ready"), 1)
                dv.wait_ge(sem("rsh_ready"), j + 1)
                if j == 0:
                    dv.wait_ge(sem("ld_gffn"), 16)
                v.scalar_tensor_tensor(out=hnr[0:n, par, :], in0=hrow[0:n, par, :], scalar=rsh[0:n, j:j + 1], in1=gffn[0:n],
                                       op0=ALU.mult, op1=ALU.mult).then_inc(sem("hn_ready"), 1)

            def logits(j):
                n, par = ROWS[j], j % 2
                dv.wait_ge(sem("lg_pe"), j + 1)
                v.tensor_tensor(lg[0:n, j, :], banks[6][0:n, 0:NE], brt[0:n, :], ALU.add).then_inc(sem("lg_ready"), 1)

            m_ = chosen[:, 0:NTT, :]

            def choose(j):
                link(v.max(top[:, j, :], lg[:, j, :]))
                link(v.max_index(tid[:, j, :], top[:, j, :], lg[:, j, :]))
                v.tensor_tensor(lm[:, j, :], lg[:, j, :], top[:, j, 0:1].broadcast_to([P, NE]), ALU.subtract).then_inc(sem("lgm_ready"), 1)
                link(v.tensor_copy(tidf[:, j, :], tid[:, j, 0:TOPK]))
                for k in range(TOPK):
                    last = v.tensor_scalar(hot4[:, j, k, :], c_("iota"), tidf[:, j, k:k + 1], c_("valid")[:, j:j + 1],
                                           ALU.is_equal, ALU.mult)
                link(last)
                v.tensor_reduce(m_[:, j, :], hot4[:, j].rearrange("p k e -> p e k"), AX.X, ALU.add).then_inc(sem("m_ready"), 1)

            for j in range(NTT):
                h_rows(j)
                if j >= 1:
                    logits(j - 1)
                h_norm(j)
                if j >= 1:
                    dv.wait_ge(sem("lg_ready"), j)
                    if j == 1:
                        v.memset(chosen[:, NTT, :], 0.0)
                    choose(j - 1)
            logits(NTT - 1)
            dv.wait_ge(sem("lg_ready"), NTT)
            choose(NTT - 1)
            v.memset(eid_i[:, EXTRA:EXTRA + 1], 0)
            v.tensor_copy(rv[:, 0, :, 0:1], c_("tokid").rearrange("p (j o) -> p j o", o=1))
            v.tensor_copy(rv[:, 1, :, 0:1], c_("tokid").rearrange("p (j o) -> p j o", o=1))
            v.memset(rv[:, :, :, 2:3], 1.0)
            v.memset(wk2, 0.0)
            dv.wait_ge(sem("m_ready"), NTT)
            dv.wait_ge(sem("gexp_ready"), 1)
            gx = wk[:, 1, :].rearrange("p (j e) -> p j e", j=NTT)
            link(v.tensor_tensor(gx, gx, m_, ALU.mult))
            gs = wk[:, 6, 0:NTT].rearrange("p (j o) -> p j o", o=1)
            link(v.tensor_reduce(gs, gx, AX.X, ALU.add))
            link(v.tensor_tensor(gs, gs, c_("valid").rearrange("p (j o) -> p j o", o=1), ALU.mult))
            inv = wk[:, 7, 0:NTT].rearrange("p (j o) -> p j o", o=1)
            link(v.tensor_scalar(inv, c_("valid").rearrange("p (j o) -> p j o", o=1), -1.0, 1.0, ALU.mult, ALU.add))
            link(v.tensor_tensor(gs, gs, inv, ALU.add))
            link(v.reciprocal(inv, gs))
            link(v.memset(gate, 0.0))
            link(v.memset(posm, -1.0))
            link(v.memset(ptab, 0.0))
            link(v.tensor_copy(ptab[:, 0:NE], c_("eye2")))
            link(v.tensor_tensor(gate[:, :, 0:NE], gx, inv.broadcast_to([P, NTT, NE]), ALU.mult))
            dv.wait_ge(sem("pos_pe"), 1)
            pos = banks[0][:, 0:160].rearrange("p (j e) -> p j e", j=NTT)
            pt = wk[:, 8, :].rearrange("p (j e) -> p j e", j=NTT)
            link(v.scalar_tensor_tensor(out=pt, in0=pos, scalar=1.0, in1=m_, op0=ALU.add, op1=ALU.mult))
            link(v.tensor_scalar(posm[:, :, 0:NE], pt, -1.0, None, ALU.add))

            def hot_slots(n, k):
                wait(dv, "info_pe", n - 1)
                wait(dv, "w_used", (n - 2) * HALVES + 9)
                v.tensor_copy(rv[:, k % 2, :, 1:2], gate[:, :, bass.ds(n, 1)])
                v.tensor_copy(pick_r[0:2 * NE, (k % 2) * CAP:(k % 2 + 1) * CAP], ptab[0:2 * NE, bass.ds(n, 1)].broadcast_to([2 * NE, CAP]))
                v.tensor_tensor(hot[:, k % 2], c_("slot").rearrange("p (o s) -> p o s", o=1).broadcast_to([P, NTT, CAP]),
                                posm[:, :, bass.ds(n, 1)].broadcast_to([P, NTT, CAP]), ALU.is_equal).then_inc(sem("hot_ready"), 1)

            hot_slots(0, 0)
            link(v.tensor_copy(cnt, banks[0][:, 160:192]))
            link(v.tensor_reduce(wk[:, 9, 0:1], cnt, AX.X, ALU.max))
            link(v.tensor_scalar(wk[:, 9, 1:2], wk[:, 9, 0:1], CAP + 0.5, None, ALU.is_gt))
            link(v.tensor_copy(flag_i[:, :], wk[:, 9, 1:2]))
            flag = dv.value_load(flag_i[0:1, 0:1], min_val=0, max_val=1)

            with dv.If(flag > 0):
                c0 = chain[0]
                nb, ci, cx, t0 = (wk[:, r, 0:NE] for r in (9, 10, 11, 6))
                link(v.tensor_scalar(nb, cnt, CAP + 0.5, None, ALU.is_gt))
                for b in range(2, BLOCKS):
                    link(v.scalar_tensor_tensor(out=nb, in0=cnt, scalar=b * CAP + 0.5, in1=nb, op0=ALU.is_gt, op1=ALU.add))
                src, dst = ci, t0
                link(v.tensor_copy(ci, nb))
                for s in (1, 2, 4, 8, 16):
                    link(v.tensor_copy(dst[:, 0:s], src[:, 0:s]))
                    link(v.tensor_tensor(dst[:, s:NE], src[:, s:NE], src[:, 0:NE - s], ALU.add))
                    src, dst = dst, src
                inc = src
                link(v.tensor_tensor(cx, inc, nb, ALU.subtract))
                sel, tmp, shf = (b[:, 0:EXTRA * NE].rearrange("p (i e) -> p i e", e=NE) for b in (big1, big2, big3))
                for i in range(EXTRA):
                    bi = c_("blk")[:, i:i + 1]
                    link(v.tensor_scalar(tmp[:, i, :], inc, bi, None, ALU.is_gt))
                    link(v.tensor_scalar(sel[:, i, :], cx, bi, None, ALU.is_le))
                    link(v.tensor_scalar(shf[:, i, :], cx, bi, float(-CAP), ALU.subtract, ALU.mult))
                link(v.tensor_tensor(sel, sel, tmp, ALU.mult))
                link(v.tensor_scalar(shf, shf, float(CAP), None, ALU.add))
                one = wk[:, 7, 0:EXTRA]
                link(v.tensor_reduce(one, sel, AX.X, ALU.add))
                link(v.tensor_scalar(one, one, -1.0, None, ALU.add))
                for j in range(NTT):
                    pj, gj = posm[:, j, NE:NE + EXTRA], gate[:, j, NE:NE + EXTRA]
                    pe_ = posm[:, j:j + 1, 0:NE].broadcast_to([P, EXTRA, NE])
                    link(v.tensor_tensor(tmp, pe_, shf, ALU.subtract))
                    link(v.tensor_tensor(tmp, tmp, sel, ALU.mult))
                    link(v.tensor_reduce(pj, tmp, AX.X, ALU.add))
                    link(v.tensor_tensor(pj, pj, one, ALU.add))
                    link(v.tensor_tensor(tmp, gate[:, j:j + 1, 0:NE].broadcast_to([P, EXTRA, NE]), sel, ALU.mult))
                    link(v.tensor_reduce(gj, tmp, AX.X, ALU.add))
                for i in range(EXTRA):
                    link(v.tensor_tensor(tmp[:, i, :], sel[:, i, :], c_("iota"), ALU.mult))
                link(v.tensor_reduce(one, tmp, AX.X, ALU.add))
                link(v.tensor_copy(eid_i[:, 0:EXTRA], one))
                link(v.tensor_tensor(tmp, sel, c_("eye2").rearrange("p (o e) -> p o e", o=1).broadcast_to([P, EXTRA, NE]), ALU.mult))
                link(v.tensor_reduce(ptab[:, NE:NE + EXTRA], tmp, AX.X, ALU.add))
                skipped = chain[0] - c0
            with dv.Else():
                v.memset(eid_i[:, 0:EXTRA], 0).then_inc(sem("dve_chain"), skipped)
            dv.wait_ge(sem("dve_chain"), chain[0])

            v.memset(mx, 0.0).then_inc(sem("route_ready"), 1)

            def slot_info(n, k):
                dv.wait_ge(sem("info_pe"), n + 1)
                wait(dv, "scattered", n * 16 - 48)
                info = banks[6][0:CAP, 416:419]
                free, t = wk2[0:CAP, 0:1], wk2[0:CAP, 1:2]
                v.tensor_scalar(free, info[:, 2:3], -1.0, 1.0, ALU.mult, ALU.add).then_inc(sem("in_a"), 1)
                v.tensor_copy(gcol[0:CAP, k % UB:k % UB + 1], info[:, 1:2])
                dv.wait_ge(sem("in_a"), n + 1)
                v.scalar_tensor_tensor(out=t, in0=free, scalar=c_("pad")[0:CAP], in1=info[:, 0:1], op0=ALU.mult, op1=ALU.add).then_inc(sem("in_b"), 1)
                dv.wait_ge(sem("in_b"), n + 1)
                v.tensor_copy(idx_i[0:CAP, k % UB:k % UB + 1], t).then_inc(sem("idx_ready"), 1)

            def x_low(n):
                for half in range(2):
                    hs = slice(half * 4, half * 4 + 4)
                    dv.wait_ge(sem("x_high"), n * 2 + (half + 1))
                    v.tensor_tensor(xL[:, hs, :], split(banks[half][:, 0:4 * CAP], 4), xH[:, hs, :], ALU.subtract).then_inc(sem("x_low"), 1)

            def act_low(n, fh):
                hs = slice(fh * 4, fh * 4 + 4)
                dv.wait_ge(sem("act_high"), n * 2 + (fh + 1))
                v.tensor_tensor(aL[:, hs, :], split(banks[6 + fh][:, 0:4 * CAP], 4), aH[:, hs, :], ALU.subtract).then_inc(sem("act_low"), 1)

            def low_part(n, t):
                parts = 1 if t in POOL_T else 2
                dv.wait_ge(sem("w_high"), n * HALVES + (t + 1))
                for part in range(parts):
                    last = v.tensor_tensor(low_w(t, part, 2), raw_w(t, part, 2), high_w(t, part, 2), ALU.subtract)
                last.then_inc(sem("w_low"), 1)

            def swiglu(n, fh):
                m = n * 2 + fh
                g, u = gt[0:CAP, fh, :], up[0:CAP, fh, :]
                dv.wait_ge(sem("w_used"), n * HALVES + 4 * fh + 4)
                v.tensor_scalar(g, banks[2 * fh][0:CAP, :], LIMIT, None, ALU.min).then_inc(sem("gate_ready"), 1)
                wait(dv, "act_pe", m - 1)
                v.tensor_scalar(u, banks[2 * fh + 1][0:CAP, :], LIMIT, -LIMIT, ALU.min, ALU.max).then_inc(sem("up_ready"), 1)
                dv.wait_ge(sem("gate_ready"), m + 1)
                dv.wait_ge(sem("up_ready"), m + 1)
                v.scalar_tensor_tensor(out=u, in0=u, scalar=1.0, in1=g, op0=ALU.add, op1=ALU.mult).then_inc(sem("prod_ready"), 1)
                dv.wait_ge(sem("prod_ready"), m + 1)
                dv.wait_ge(sem("sig_ready"), m + 1)
                v.tensor_tensor(u, u, sg[0:CAP, fh, :], ALU.mult).then_inc(sem("act_ready"), 1)

            def ahead(t):
                return {7: (), 8: (10, 11), 9: (), 10: (12, 13)}.get(t, (t + LEAD,))

            def expert(n, k):
                for t in range(HALVES):
                    if t == 0:
                        hot_slots(n + 1, k + 1)
                    if t == 2:
                        slot_info(n + 1, k + 1)
                    if t in (4, 8):
                        swiglu(n, (t - 4) // 4)
                    if t in (6, 10):
                        act_low(n, (t - 6) // 4)
                    if t == 10:
                        x_low(n + 1)
                    for lead in ahead(t):
                        low_part(n + lead // HALVES, lead % HALVES)

            slot_info(0, 0)
            for t in range(LEAD):
                low_part(0, t)
            x_low(0)
            for u in range(UB):
                expert(u, u)
            with dv.Fori(1, NE // UB) as it:
                for u in range(UB):
                    expert(it * UB + u, u)
            with dv.If(flag > 0):
                with dv.Fori(0, EXTRA // UB) as it:
                    for u in range(UB):
                        expert(it * UB + (NE + u), u)
            dv.wait_ge(sem("ld_gf"), 16)
            for j in range(NTT):
                n = ROWS[j]
                dv.wait_ge(sem("ssf_raw"), j + 1)
                v.tensor_scalar(ssf[0:n, j:j + 1], ssf[0:n, j:j + 1], 1.0 / D, EPS, ALU.mult, ALU.add).then_inc(sem("ssf_ready"), 1)
                dv.wait_ge(sem("rsf_ready"), j + 1)
                v.scalar_tensor_tensor(out=yf[0:n, j, :], in0=yf[0:n, j, :], scalar=rsf[0:n, j:j + 1], in1=gfin[0:n],
                                       op0=ALU.mult, op1=ALU.mult).then_inc(sem("yf_ready"), 1)

        @block.tensor
        def _(pe):
            mm, tr = nc.tensor.matmul, nc.tensor.transpose
            pe.wait_ge(sem("ld_cst"), 16)
            for r in range(7):
                ap, n = row_tile(r)
                pe.wait_ge(sem("xn_ready"), r + 1)
                if r >= 2:
                    pe.wait_ge(sem("xT_ready"), 2 * r - 2)
                for half in range(2):
                    for k in range(4):
                        kk = half * 4 + k
                        last = tr(banks[2 * (r % 2) + half][:, k * P:k * P + n], ap[:, kk * P:(kk + 1) * P], ident[0:n, 0:n])
                    last.then_inc(sem("xT_pe"), 1)
            pe.wait_ge(sem("ld_wm"), 16)
            pe.wait_ge(sem("xT_ready"), 4)
            for m in range(2):
                for k in range(KD):
                    last = mm(banks[5 + m][:, :], memT[:, k, m * P:(m + 1) * P], wm[:, k, :], start=(k == 0), stop=(k == KD - 1))
                last.then_inc(sem("mkv_pe"), 1)
            for m in range(2):
                pe.wait_ge(sem("mkv_ready"), m + 1)
                for c in range(2):
                    last = tr(banks[7][:, c * 256 + m * P:c * 256 + (m + 1) * P], mkv[:, m, c * P:(c + 1) * P], ident)
            last.then_inc(sem("mkT_pe"), 1)
            pe.wait_ge(sem("ld_wi0"), 16)
            pe.wait_ge(sem("xT_ready"), 14)

            def w_tile(t, k):
                return wi[:, k, WCOL[t]:WCOL[t] + P]

            def z_half(i, half):
                job = 2 * i + half
                bank = job % 8 if job < NZ1 else 6 + half
                if job == 7:
                    pe.wait_ge(sem("mkT_ready"), 1)
                if 8 <= job < NZ1:
                    pe.wait_ge(sem("z_act" if half else "z_dve"), i - 3)
                if job >= NZ1:
                    pe.wait_ge(sem("z_act" if half else "z_dve"), i)
                for k in range(KD):
                    last = mm(banks[bank][:, 0:HALF], w_tile(Z_ORDER[i], k), xT0[:, k, half * HALF:(half + 1) * HALF],
                              start=(k == 0), stop=(k == KD - 1))
                last.then_inc(sem("z_pe"), 1)

            for i in range(len(Z_FIRST)):
                z_half(i, 0)
                z_half(i, 1)
            for j in range(NTT):
                c0 = P if j < 3 else 0
                job = NZ1 + j
                pe.wait_ge(sem("z_act" if job % 2 else "z_dve"), (job - 8) // 2 + 1)
                for k in range(KD):
                    last = mm(banks[job % 8][0:ROWS[j], c0:256], xT0[:, k, j * P:j * P + ROWS[j]],
                              wi[:, k, 512 + c0:768], start=(k == 0), stop=(k == KD - 1))
                last.then_inc(sem("kvr_pe"), 1)
            pe.wait_ge(sem("kvr_act"), 2)
            pe.wait_ge(sem("kvr_dve"), 3)
            pe.wait_ge(sem("z_act"), len(Z_FIRST))
            pe.wait_ge(sem("z_dve"), len(Z_FIRST))

            def scores(i):
                kind, n, nh, w = UNITS[i]
                if kind == "swa":
                    if n > 0:
                        pe.wait_ge(sem("negm_ready"), i)
                    for t in range(4):
                        for g in range(2):
                            rows = slice(g * HD, (g + 1) * HD)
                            last = mm(swa_psum(n, g * 4 + t), zT[rows, t, n * P:(n + 1) * P],
                                      zT[rows, 8, (n + 1) * P - w:(n + 1) * P], start=True, stop=True)
                elif kind == "mem":
                    pe.wait_ge(sem("negm_ready"), 4)
                    pe.wait_ge(sem("z_dve"), len(Z_ORDER))
                    pe.wait_ge(sem("z_act"), len(Z_ORDER))
                    if i >= 6:
                        pe.wait_ge(sem("exp_ready"), i - 1)
                    for h in range(4):
                        rows = slice((h % 2) * HD, (h % 2 + 1) * HD)
                        last = mm(banks[S_BANK[i] + h % 2][:, (h // 2) * 256:(h // 2 + 1) * 256],
                                  zT[rows, 6 + h // 2, n * P:(n + 1) * P], mkT[rows, h // 2, :], start=True, stop=True)
                elif kind == "sswa":
                    pe.wait_ge(sem("st8_ready"), 1)
                    for r in range(2):
                        tr(banks[0][:, r * 160:r * 160 + P], ST[:, r * P:(r + 1) * P], ident)
                        last = mm(banks[0][:, r * 160 + P:(r + 1) * 160], qbd[:, 4 * r:4 * r + 4].rearrange("p b v n -> p (b v n)"),
                                  zT[:, 8, NPR:NT], start=True, stop=True)
                else:
                    pe.wait_ge(sem("st9_ready"), 1)
                    for half in range(2):
                        last = tr(banks[2][:, half * P:(half + 1) * P], ST[:, half * P:(half + 1) * P], ident)
                last.then_inc(sem("s_pe"), 1)

            def job_bank(j):
                if j >= 2:
                    pe.wait_ge(sem("job_out"), j - 1)
                return banks[4 + j % 2]

            def outputs(i):
                kind, n, nh, w = UNITS[i]
                s, j = s_view(i), JB[i]
                pe.wait_ge(sem("p_ready"), i + 1)
                halves = [1] if (kind, n) == ("swa", 0) else [0, 1]
                if kind == "swa":
                    for g in range(2):
                        for half in halves:
                            bank = job_bank(j)
                            off = (half * P) if w == 256 else 0
                            for t in range(4):
                                last = tr(bank[:, t * P:(t + 1) * P], s[:, g * 4 + t, off:off + P], ident)
                            last.then_inc(sem("job_pe"), 1)
                            j += 1
                    bank = job_bank(j)
                    pe.wait_ge(sem("job_out"), j)
                    for g in range(2):
                        for half in halves:
                            last = mm(bank[g * HD:(g + 1) * HD, :], kvr[:, n - 1 + half, P + g * HD:P + (g + 1) * HD],
                                      pT[:, g * 2 + half, :], start=(half == halves[0]), stop=(half == 1))
                elif kind == "mem":
                    for half in halves:
                        bank = job_bank(j)
                        for h in range(4):
                            last = tr(bank[:, h * P:(h + 1) * P], s[:, (h % 2) * 2 + h // 2, half * P:(half + 1) * P], ident)
                        last.then_inc(sem("job_pe"), 1)
                        j += 1
                    bank = job_bank(j)
                    pe.wait_ge(sem("job_out"), j)
                    for h in range(4):
                        for half in halves:
                            last = mm(bank[(h % 2) * HD:(h % 2 + 1) * HD, (h // 2) * P:(h // 2 + 1) * P],
                                      mkv[:, half, 256 + h * HD:256 + (h + 1) * HD], pT[:, half, h * P:(h + 1) * P],
                                      start=(half == 0), stop=(half == 1))
                elif kind == "sswa":
                    bank = job_bank(j)
                    for r in range(2):
                        tr(bank[:, r * P:(r + 1) * P], s[:, r, 0:P], ident)
                        last = tr(bank[0:32, 256 + r * P:256 + (r + 1) * P], s[:, r, P:160], ident)
                    last.then_inc(sem("job_pe"), 1)
                    j += 1
                    bank = job_bank(j)
                    pe.wait_ge(sem("job_out"), j)
                    pe.wait_ge(sem("ld_vc"), 16)
                    for b in range(NB):
                        cols = slice(b * 32, (b + 1) * 32)
                        mm(bank[:, cols], kvr[0:32, 4, P:256], pT[0:32, 1, cols], start=True, stop=False)
                        last = mm(bank[:, cols], vc[:, b, :], pT[:, 0, cols], start=False, stop=True)
                else:
                    bank = job_bank(j)
                    for half in range(2):
                        last = tr(bank[:, half * P:(half + 1) * P], s[:, 0, half * P:(half + 1) * P], ident)
                    last.then_inc(sem("job_pe"), 1)
                    j += 1
                    bank = job_bank(j)
                    pe.wait_ge(sem("job_out"), j)
                    pe.wait_ge(sem("ld_mcv"), 16)
                    for b in range(NB):
                        for c in range(2):
                            col = (b * 2 + c) * 8
                            for half in range(2):
                                last = mm(bank[:, col:col + 8], mcv[:, b, half, c * P:(c + 1) * P],
                                          pT[:, 0, half * P + col:half * P + col + 8], start=(half == 0), stop=(half == 1))
                last.then_inc(sem("job_pe"), 1)

            zi = len(Z_FIRST)
            scores(0)
            pe.wait_ge(sem("ld_wi768"), 16)
            for i in range(NU):
                if i < 4:
                    for _ in Z_LATER[i]:
                        z_half(zi, 0)
                        z_half(zi, 1)
                        zi += 1
                if i == 4:
                    pe.wait_ge(sem("z_dve"), len(Z_ORDER))
                    pe.wait_ge(sem("z_act"), len(Z_ORDER))
                    pe.wait_ge(sem("diag_ready"), 1)
                    for c in range(2):
                        last = tr(banks[7][0:18, 256 + c * P:256 + (c + 1) * P], ul[:, c, :], ident)
                    last.then_inc(sem("ul_pe"), 1)
                if i == 7:
                    pe.wait_ge(sem("ld_kc"), 16)
                    pe.wait_ge(sem("exp_ready"), 7)
                    for b in range(NB):
                        last = mm(banks[1][:, b * 32:(b + 1) * 32], kcT[:, b, :], qbd[:, b].rearrange("p v n -> p (v n)"),
                                  start=True, stop=True)
                    last.then_inc(sem("st8_pe"), 1)
                if i == 8:
                    pe.wait_ge(sem("ld_mck"), 16)
                    pe.wait_ge(sem("exp_ready"), 8)
                    for b in range(NB):
                        for c in range(2):
                            for half in range(2):
                                col = half * P + (b * 2 + c) * 8
                                last = mm(banks[3][:, col:col + 8], mckT[:, c, b, half * P:(half + 1) * P],
                                          mqbd[:, c, b, :], start=True, stop=True)
                    last.then_inc(sem("st9_pe"), 1)
                if i + 1 < NU:
                    scores(i + 1)
                outputs(i)
            pe.wait_ge(sem("job_out"), JB[NU])

            def square_sums():
                pe.wait_ge(sem("sq_sums"), 1)
                for j in range(NTT):
                    n = ROWS[j]
                    for part, tiles in enumerate(PARTS):
                        last = mm(banks[6][0:n, j * 3 + part:j * 3 + part + 1], sq[:, tiles[0], j * P:j * P + n],
                                  c_("ones")[:, 0:1], start=True, stop=True)
                    last.then_inc(sem("sq_pe"), 1)

            pe.wait_ge(sem("ld_wo"), 16)

            def router_rows(j):
                n, par = ROWS[j], j % 2
                pe.wait_ge(sem("hn_ready"), j + 1)
                if j == 0:
                    pe.wait_ge(sem("ss3_ready"), 1)
                else:
                    pe.wait_ge(sem("lg_ready"), j)
                for half in range(2):
                    for k in range(4):
                        kk = half * 4 + k
                        last = tr(banks[6 + half][:, k * P:k * P + n], hnr[0:n, par, kk * P:(kk + 1) * P], ident[0:n, 0:n])
                    last.then_inc(sem("hT_pe"), 1)

            def router(j):
                n, par = ROWS[j], j % 2
                pe.wait_ge(sem("hT_ready"), 2 * j + 2)
                for k in range(KD):
                    last = mm(banks[6][0:n, 0:NE], hnT[:, par, k, 0:n], wr[:, k, :], start=(k == 0), stop=(k == KD - 1))
                last.then_inc(sem("lg_pe"), 1)

            for j in range(NTT):
                n = ROWS[j]
                for half in range(2):
                    if half == 1:
                        if j == 0:
                            square_sums()
                        else:
                            router_rows(j - 1)
                    for part, tiles in enumerate(PARTS):
                        if j >= 1:
                            pe.wait_ge(sem("h_ready"), 2 * j - 1 + half)
                        for t in tiles:
                            if j == 0 and half == 0:
                                pe.wait_ge(sem("mix_ready"), t + 1)
                            last = mm(banks[half * 3 + part][0:n, :], zT[:, t, j * P:j * P + n], wo[:, t, half * 512:(half + 1) * 512],
                                      start=(t == tiles[0]), stop=(t == tiles[-1]))
                        last.then_inc(sem("h_pe"), 1)
                if j >= 1:
                    router(j - 1)
            router_rows(NTT - 1)
            router(NTT - 1)
            pe.wait_ge(sem("m_ready"), NTT)
            mm(split(banks[0][:, 0:(NTT + 1) * NE], NTT + 1), c_("tri"), chosen, start=True, stop=False, skip_group_check=True)
            for i in range(NTT):
                last = mm(split(banks[0][:, (i + 1) * NE:(NTT + 1) * NE], NTT - i), c_("ones"),
                          chosen[:, i:i + 1, :].broadcast_to([P, NTT - i, NE]), start=False, stop=(i == NTT - 1), skip_group_check=True)
            last.then_inc(sem("pos_pe"), 1)


            def info(n, k):
                pe.wait_ge(sem("hot_ready"), n + 1)
                wait(pe, "act_low", n * 2 - 3)
                for j in range(NTT):
                    last = mm(banks[6][0:CAP, 416:419], hot[:, k % 2, j, :], rv[:, k % 2, j, :], start=(j == 0), stop=(j == NTT - 1))
                last.then_inc(sem("info_pe"), 1)

            def x_rows(n, k):
                pe.wait_ge(sem("gathered"), n * 16 + 16)
                wait(pe, "up_ready", n * 2 - 1)
                for half in range(2):
                    for q in range(4):
                        kk = half * 4 + q
                        last = tr(banks[half][:, q * CAP:(q + 1) * CAP], xg[0:CAP, k % 2, kk * P:(kk + 1) * P], ident[0:CAP, 0:CAP])
                    last.then_inc(sem("xg_pe"), 1)

            def act_rows(n, fh):
                pe.wait_ge(sem("act_ready"), n * 2 + (fh + 1))
                if fh == 0:
                    pe.wait_ge(sem("idx_ready"), n + 2)
                for q in range(4):
                    last = tr(banks[6 + fh][:, q * CAP:(q + 1) * CAP], up[0:CAP, fh, q * P:(q + 1) * P], ident[0:CAP, 0:CAP])
                last.then_inc(sem("act_pe"), 1)

            def split_done(n, t):
                pe.wait_ge(sem("w_low"), n * HALVES + (t + 1))
                if t in POOL_T:
                    pe.wait_ge(sem("w_low_pool"), n * len(POOL_T) + (POOL_T.index(t) + 1))

            def products(bank, high, low, wh, wl, stop):
                mm(bank, high, wh, start=False, stop=False)
                mm(bank, low, wh, start=False, stop=False)
                return mm(bank, high, wl, start=False, stop=stop)

            def expert(n, k):
                pick = pick_r[0:2 * NE, (k % 2) * CAP:(k % 2 + 1) * CAP]
                for t in range(8):
                    q = t // 2
                    bank = banks[q][0:CAP, :]
                    if t == 0:
                        pe.wait_ge(sem("x_low"), n * 2 + 2)
                    if t == 4:
                        wait(pe, "up_ready", n * 2)
                    if t % 2 == 0:
                        mm(bank, pick, bias_r[0:2 * NE, q * 512:(q + 1) * 512], start=True, stop=False)
                    split_done(n, t)
                    wh, wl = split(high_w(t), 4), split(low_w(t), 4)
                    for i in range(4):
                        kk = (t % 2) * 4 + i
                        last = products(bank, xH[:, kk, :], xL[:, kk, :], wh[:, i, :], wl[:, i, :], kk == KD - 1)
                    last.then_inc(sem("w_used"), 1)
                    if t == 1:
                        info(n + 1, k + 1)
                    if t == 5:
                        act_rows(n, 0)
                wait(pe, "yrow_ready", n * 2)
                for dh in range(2):
                    mm(banks[4 + dh][0:CAP, :], pick, bias_r[0:2 * NE, 2048 + dh * 512:2048 + (dh + 1) * 512], start=True, stop=False)
                for t in range(8, HALVES):
                    f0 = (t - 8) * 2
                    if f0 % 4 == 0:
                        pe.wait_ge(sem("act_low"), n * 2 + (f0 // 4 + 1))
                    split_done(n, t)
                    wh, wl = split(high_w(t), 2), split(low_w(t), 2)
                    for i in range(2):
                        for dh in range(2):
                            cols = slice(dh * 512, (dh + 1) * 512)
                            last = products(banks[4 + dh][0:CAP, :], aH[:, f0 + i, :], aL[:, f0 + i, :], wh[:, i, cols], wl[:, i, cols],
                                            f0 + i == KD - 1)
                        if t == 9 and i == 0:
                            act_rows(n, 1)
                    last.then_inc(sem("w_used"), 1)
                    if t == 9:
                        x_rows(n + 1, k + 1)

            info(0, 0)
            pe.wait_ge(sem("route_ready"), 1)
            flag = pe.value_load(flag_i[0:1, 0:1], min_val=0, max_val=1)
            x_rows(0, 0)
            for u in range(UB):
                expert(u, u)
            with pe.Fori(1, NE // UB) as it:
                for u in range(UB):
                    expert(it * UB + u, u)
            with pe.If(flag > 0):
                with pe.Fori(0, EXTRA // UB) as it:
                    for u in range(UB):
                        expert(it * UB + (NE + u), u)


def laid_out(x):
    cols = lambda a: a.reshape(-1, P).T
    heads = lambda a: a.reshape(2, 4, HD, -1).transpose(1, 0, 2, 3).reshape(512, -1)
    w_in, w_out, g_mix = x["w_in"][0], x["w_out"][0], x["g_mix_out"][0]
    return {
        "x_prompt": x["x_prompt"], "x_sample": x["x_sample"], "mem_prompt": x["mem_prompt"],
        "cache_win_k": x["cache_win_k"], "cache_win_v": x["cache_win_v"],
        "win_kT": x["cache_win_k"][0].transpose(2, 3, 0, 1).reshape(P, NB, WIN),
        "mem_kT": x["cache_mem_k"][0].transpose(2, 3, 0, 1).reshape(2, P, NB, NMEM).transpose(1, 0, 2, 3),
        "cache_mem_v": x["cache_mem_v"],
        "vectors": np.concatenate([cols(x["g_attn_norm"]), cols(x["g_mem_norm"]),
                                   cols(np.concatenate([heads(g_mix[:512, None])[:, 0], g_mix[512:]])),
                                   cols(x["conv_w"]), cols(x["state_conv"])], axis=1),
        "w_in": np.concatenate([heads(w_in.T[:512]).T, w_in[:, 512:]], axis=1),
        "attn_sinks": x["attn_sinks"], "w_mem_kv": x["w_mem_kv"],
        "w_out": np.concatenate([heads(w_out[:512]), w_out[512:]], axis=0),
        "g_ffn": x["g_ffn_norm"], "w_router": x["w_router"], "b_router": x["b_router"],
        "w_gate_up": x["w_gate_up"].reshape(NE, KD, P, 2, 512, 2).transpose(0, 3, 5, 2, 1, 4).reshape(NE * 4, P, CHW),
        "w_down": x["w_down"].reshape(NE, 2, 4, P, D).transpose(0, 1, 3, 2, 4).reshape(NE * 2, P, CHW),
        "biases": np.concatenate([x["b_gate_up"].reshape(NE, 2, 512, 2).transpose(0, 1, 3, 2).reshape(NE, 2 * D),
                                  x["b_down"].reshape(NE, D)], axis=1),
        "g_final": x["g_final"],
    }


_OUTS = [(1, NPR, D), (NB, TS, D), (1, 1, WIN, 2, HD), (1, 1, WIN, 2, HD), (1, 1, 2, 256), (1, 1, NMEM, 4, HD),
         (1, 1, NMEM, 4, HD), (1, NB, WIN, 2, HD), (1, NB, WIN, 2, HD), (1, NB, 2, 256)]


def kernel(**inputs):
    import concourse.bacc as bacc
    from concourse.bass_utils import run_bass_kernel_spmd

    nc = bacc.Bacc("TRN2", target_bir_lowering=False, num_devices=1)
    arrays, args = {}, []
    for name, a in laid_out({k: np.asarray(v) for k, v in inputs.items()}).items():
        a = np.ascontiguousarray(a)
        arrays[f"in_{name}"] = a
        args.append(nc.dram_tensor(f"in_{name}", a.shape, mybir.dt.from_np(a.dtype), kind="ExternalInput").ap())
    for i, shape in enumerate(_OUTS):
        args.append(nc.dram_tensor(f"out_{i}", shape, F32, kind="ExternalOutput").ap())
    build(nc, *args)
    r = run_bass_kernel_spmd(nc, [arrays], core_ids=[0])
    return tuple(r.results[0][f"out_{i}"] for i in range(len(_OUTS)))
```
